# Optimizing a Trainium2 kernel written in Bass

```python
import jax, jax.numpy as jnp
from jax import lax
import numpy as np

D_MODEL = 1024
BATCH = 1
SEQ = 512
DEPTH = 2
DEC_BATCH = 8
DEC_SEQ = 8
PAST_LEN = 4096
PAGE_SIZE = 128

N_A_LAYERS = (DEPTH + 1) // 2
N_C_LAYERS = DEPTH // 2

POOL_WINDOWS = (2, 4, 8, 16)
POOL_GROUPS = len(POOL_WINDOWS)
POOL_WIDTH = D_MODEL // 2
POOL_GW = POOL_WIDTH // POOL_GROUPS
POOL_BUF = max(POOL_WINDOWS) - 1
MLSTM_HEADS = 4
MLSTM_WIDTH = D_MODEL // 2
MLSTM_HD = MLSTM_WIDTH // MLSTM_HEADS
MLSTM_CHUNK = 64
CONV_W = 4
MIX_A = POOL_WIDTH + MLSTM_WIDTH
IN_A = 2 * POOL_WIDTH + 5 * MLSTM_WIDTH + 2 * MLSTM_HEADS
NSA_HEADS = 16
NSA_HD = D_MODEL // NSA_HEADS
NSA_KV = 4
NSA_REP = NSA_HEADS // NSA_KV
NSA_WIDTH = NSA_HEADS * NSA_HD
KVW = NSA_KV * NSA_HD
IN_C = NSA_WIDTH + 6 * KVW + 3 * NSA_HEADS + NSA_WIDTH
CMP_STRIDE = 16
CMP_BLOCK = 2 * CMP_STRIDE
SEL_BLOCK = 64
SEL_TOP = 16
WINDOW = 512
ROPE_THETA = 500000.0
ROPE_DIM = NSA_HD // 4
Q_BLOCK = 16
NEG = -1e30
FORCE = 1e4
EPS = 1e-6

kernel_name = "hybrid_pool_mlstm_nsa_decode_step"

def rmsnorm(x, g):
    xf = x.astype(jnp.float32)
    y = xf * lax.rsqrt(jnp.mean(xf * xf, axis=-1, keepdims=True) + EPS)
    return (y * g.astype(jnp.float32)).astype(x.dtype)

def ada_mod(c, w, b):
    m = jnp.einsum('bd,de->be', jax.nn.silu(c), w) + b
    shift, scale, gate = jnp.split(m, 3, axis=-1)
    return shift[:, None], scale[:, None], gate[:, None]

def rope_partial(x, pos):
    half = ROPE_DIM // 2
    freq = jnp.power(ROPE_THETA, -2.0 * jnp.arange(half, dtype=jnp.float32) / ROPE_DIM)
    ang = pos.astype(jnp.float32)[:, None] * freq[None, :]
    shape = (1, ang.shape[0]) + (1,) * (x.ndim - 3) + (half,)
    cos, sin = jnp.cos(ang).reshape(shape), jnp.sin(ang).reshape(shape)
    xf = x.astype(jnp.float32)
    x1, x2 = xf[..., :half], xf[..., half:ROPE_DIM]
    out = jnp.concatenate([x1 * cos - x2 * sin, x2 * cos + x1 * sin, xf[..., ROPE_DIM:]], axis=-1)
    return out.astype(x.dtype)

def masked_softmax(s, mask):
    s = jnp.where(mask, s.astype(jnp.float32), NEG)
    m = jnp.max(s, axis=-1, keepdims=True)
    p = jnp.where(mask, jnp.exp(s - m), 0.0)
    return p / jnp.maximum(jnp.sum(p, axis=-1, keepdims=True), 1e-30)

def pool_mix(xp, buf, pos0, w_grp, scale):
    B, T, _ = xp.shape
    xc = jnp.concatenate([buf.astype(xp.dtype), xp], axis=1)
    xf = xc.astype(jnp.float32)
    cs = jnp.concatenate([jnp.zeros_like(xf[:, :1]), jnp.cumsum(xf, axis=1)], axis=1)
    end = cs[:, POOL_BUF + 1:]
    pos = pos0 + jnp.arange(T)
    means = []
    for g, w in enumerate(POOL_WINDOWS):
        sl = slice(g * POOL_GW, (g + 1) * POOL_GW)
        start = cs[:, POOL_BUF + 1 - w:POOL_BUF + 1 - w + T, sl]
        cnt = jnp.minimum(pos + 1, w).astype(jnp.float32)[None, :, None]
        means.append((end[..., sl] - start) / cnt)
    d = (jnp.concatenate(means, axis=-1) - xp.astype(jnp.float32)).reshape(B, T, POOL_GROUPS, POOL_GW)
    y = jnp.einsum('btgi,gio->btgo', d, w_grp.astype(jnp.float32)).reshape(B, T, POOL_WIDTH) * scale.astype(jnp.float32)
    return y.astype(xp.dtype), xc[:, T:]

def causal_conv(x, buf, w, b):
    T = x.shape[1]
    xc = jnp.concatenate([buf.astype(x.dtype), x], axis=1)
    y = b + sum(xc[:, j:j + T] * w[j] for j in range(CONV_W))
    return y, xc[:, T:]

def mlstm_chunkwise(q, k, v, ig, lf, C0, n0, m0):
    B, H, T, _ = q.shape
    L = min(MLSTM_CHUNK, T)
    nc = T // L

    def chunks(a):
        return jnp.moveaxis(a.reshape((B, H, nc, L) + a.shape[3:]), 2, 0)

    causal = jnp.tril(jnp.ones((L, L), bool))

    def step(carry, xs):
        C, n, m = carry
        qc, kc, vc, ic, fc = xs
        b = jnp.cumsum(fc, axis=-1)
        a_inter = b + m[..., None]
        Dm = jnp.where(causal, b[..., :, None] - b[..., None, :] + ic[..., None, :], -jnp.inf)
        mt = jnp.maximum(a_inter, jnp.max(Dm, axis=-1))
        w_inter = jnp.exp(a_inter - mt)
        s = jnp.einsum('bhtd,bhsd->bhts', qc, kc) * jnp.exp(Dm - mt[..., None])
        num = w_inter[..., None] * jnp.einsum('bhtd,bhde->bhte', qc, C) + jnp.einsum('bhts,bhse->bhte', s, vc)
        den = w_inter * jnp.einsum('bhtd,bhd->bht', qc, n) + jnp.sum(s, axis=-1)
        h = num / jnp.maximum(jnp.abs(den), jnp.exp(-mt))[..., None]
        bl = b[..., -1]
        g = bl[..., None] - b + ic
        m_new = jnp.maximum(bl + m, jnp.max(g, axis=-1))
        decay = jnp.exp(bl + m - m_new)
        wg = jnp.exp(g - m_new[..., None])
        C_new = decay[..., None, None] * C + jnp.einsum('bhs,bhsd,bhse->bhde', wg, kc, vc)
        n_new = decay[..., None] * n + jnp.einsum('bhs,bhsd->bhd', wg, kc)
        return (C_new, n_new, m_new), h

    (C, n, m), hs = lax.scan(step, (C0, n0, m0), (chunks(q), chunks(k), chunks(v), chunks(ig), chunks(lf)))
    return jnp.moveaxis(hs, 0, 2).reshape(B, H, T, -1), C, n, m

def layer_a(x, c, pos0, pool_buf, conv_buf, C0, n0, m0,
            norm_w, ada_w, ada_b, w_in, b_if, pool_w, pool_scale, conv_w, conv_b, head_norm, w_out):
    B, T, _ = x.shape
    shift, scale, gate = ada_mod(c, ada_w, ada_b)
    h = rmsnorm(x, norm_w) * (1 + scale) + shift
    u = jnp.einsum('btd,de->bte', h, w_in)
    P, M, H = POOL_WIDTH, MLSTM_WIDTH, MLSTM_HEADS
    xpool, zpool, qk, v, o, z, gif = jnp.split(u, [P, 2 * P, 2 * P + 2 * M, 2 * P + 3 * M, 2 * P + 4 * M, 2 * P + 5 * M], axis=-1)
    y_pool, new_pool = pool_mix(xpool, pool_buf, pos0, pool_w, pool_scale)
    y_pool = y_pool * jax.nn.silu(zpool)
    qk, new_conv = causal_conv(qk, conv_buf, conv_w, conv_b)
    q, k = jnp.split(jax.nn.silu(qk), 2, axis=-1)

    def heads(a):
        return a.astype(jnp.float32).reshape(B, T, H, MLSTM_HD).transpose(0, 2, 1, 3)

    gif = gif.astype(jnp.float32) + b_if.astype(jnp.float32)
    ig = gif[..., :H].transpose(0, 2, 1)
    lf = jax.nn.log_sigmoid(gif[..., H:]).transpose(0, 2, 1)
    hm, C, n, m = mlstm_chunkwise(heads(q), heads(k) * (MLSTM_HD ** -0.5), heads(v), ig, lf,
                                  C0.astype(jnp.float32), n0.astype(jnp.float32), m0.astype(jnp.float32))
    hm = hm.transpose(0, 2, 1, 3)
    hm = hm * lax.rsqrt(jnp.mean(hm * hm, axis=-1, keepdims=True) + EPS)
    hm = hm.reshape(B, T, M) * head_norm.astype(jnp.float32)
    y_m = (hm * jax.nn.sigmoid(o.astype(jnp.float32)) * jax.nn.silu(z.astype(jnp.float32))).astype(x.dtype)
    y = jnp.einsum('bte,ed->btd', jnp.concatenate([y_pool, y_m], axis=-1), w_out)
    return x + gate * y, new_pool, new_conv, C, n, m

def compress(rows, w_pos, w1, b1, w2):
    B, S = rows.shape[:2]
    n_sub = S // CMP_STRIDE
    r = rows[:, :n_sub * CMP_STRIDE].reshape(B, n_sub, CMP_STRIDE, NSA_KV, NSA_HD)
    lo = jnp.einsum('bnigd,i->bngd', r, w_pos[:CMP_STRIDE])
    hi = jnp.einsum('bnigd,i->bngd', r, w_pos[CMP_STRIDE:])
    pooled = lo[:, :-1] + hi[:, 1:]
    hid = jax.nn.gelu(jnp.einsum('bngd,de->bnge', pooled, w1) + b1)
    return jnp.einsum('bnge,ef->bngf', hid, w2)

def compressed_kv(k_rows, v_rows, kpos, kw1, kb1, kw2, vpos, vw1, vb1, vw2):
    kc = compress(k_rows, kpos, kw1, kb1, kw2)
    vc = compress(v_rows, vpos, vw1, vb1, vw2)
    c_end = jnp.arange(kc.shape[1]) * CMP_STRIDE + CMP_BLOCK - 1
    return rope_partial(kc, c_end), vc, c_end

def cmp_to_sel(n_cmp, n_sel):
    cs = np.arange(n_cmp)[:, None] * CMP_STRIDE
    ss = np.arange(n_sel)[None, :] * SEL_BLOCK
    return jnp.asarray((cs < ss + SEL_BLOCK) & (cs + CMP_BLOCK > ss), jnp.float32)

def nsa_attend(q, qpos, gates, kc, vc, c_end, overlap, fetch_sel, kw, vw, kw_pos):
    sc = NSA_HD ** -0.5
    Bq, Tq, G, R = q.shape[:4]
    mask_c = (c_end[None, :] <= qpos[:, None])[None, :, None, None, :]
    p_c = masked_softmax(jnp.einsum('btgrd,bngd->btgrn', q, kc) * sc, mask_c)
    o_c = jnp.einsum('btgrn,bngd->btgrd', p_c, vc.astype(jnp.float32))
    imp = jnp.einsum('btgn,ns->btgs', p_c.sum(3), overlap)
    n_sel = overlap.shape[1]
    blk = jnp.arange(n_sel)[None, :]
    cur = (qpos // SEL_BLOCK)[:, None]
    valid = (blk <= cur)[None, :, None, :]
    forced = ((blk == 0) | (blk == cur) | (blk == cur - 1))[None, :, None, :]
    score = jnp.where(valid, imp + jnp.where(forced, FORCE, 0.0), NEG)
    top_val, top_idx = lax.top_k(score, min(SEL_TOP, n_sel))
    ok = top_val > 0.5 * NEG
    K = top_idx.shape[-1]
    ks, vs = fetch_sel(top_idx)
    kpos = top_idx[..., None] * SEL_BLOCK + jnp.arange(SEL_BLOCK)
    mask_s = ok[..., None] & (kpos <= qpos[None, :, None, None, None])
    s_s = jnp.einsum('btgrd,btgkjd->btgrkj', q, ks) * sc
    p_s = masked_softmax(s_s.reshape(Bq, Tq, G, R, K * SEL_BLOCK), mask_s.reshape(Bq, Tq, G, 1, K * SEL_BLOCK))
    o_s = jnp.einsum('btgrm,btgmd->btgrd', p_s, vs.reshape(Bq, Tq, G, K * SEL_BLOCK, NSA_HD).astype(jnp.float32))
    kp, qp = kw_pos[None, :], qpos[:, None]
    mask_w = ((kp <= qp) & (kp > qp - WINDOW) & (kp >= 0))[None, :, None, None, :]
    p_w = masked_softmax(jnp.einsum('btgrd,bsgd->btgrs', q, kw) * sc, mask_w)
    o_w = jnp.einsum('btgrs,bsgd->btgrd', p_w, vw.astype(jnp.float32))
    g = gates.astype(jnp.float32)
    return g[..., 0, None] * o_c + g[..., 1, None] * o_s + g[..., 2, None] * o_w

def nsa_inputs(x, c, pos, norm_w, ada_w, ada_b, w_in, b_gate):
    B, T, _ = x.shape
    shift, scale, gate = ada_mod(c, ada_w, ada_b)
    h = rmsnorm(x, norm_w) * (1 + scale) + shift
    u = jnp.einsum('btd,de->bte', h, w_in)
    cuts = np.cumsum([NSA_WIDTH] + [KVW] * 6 + [3 * NSA_HEADS]).tolist()
    q, kc, vc, ks, vs, kw, vw, g, z = jnp.split(u, cuts, axis=-1)

    def kv(a):
        return a.reshape(B, T, NSA_KV, NSA_HD)

    q = rope_partial(q.reshape(B, T, NSA_KV, NSA_REP, NSA_HD), pos)
    gates = jax.nn.sigmoid((g + b_gate).reshape(B, T, NSA_KV, NSA_REP, 3))
    return q, kv(kc), kv(vc), rope_partial(kv(ks), pos), kv(vs), rope_partial(kv(kw), pos), kv(vw), gates, z, gate

def nsa_output(x, o, z, gate, w_out):
    B, T = x.shape[:2]
    y = (o.reshape(B, T, NSA_WIDTH) * jax.nn.silu(z.astype(jnp.float32))).astype(x.dtype)
    return x + gate * jnp.einsum('bte,ed->btd', y, w_out)

def layer_c_prompt(x, c, norm_w, ada_w, ada_b, w_in, b_gate,
                   kpos, kw1, kb1, kw2, vpos, vw1, vb1, vw2, w_out):
    B, T, _ = x.shape
    pos = jnp.arange(T)
    q, kcr, vcr, ks, vs, kw, vw, gates, z, gate = nsa_inputs(x, c, pos, norm_w, ada_w, ada_b, w_in, b_gate)
    kc, vc, c_end = compressed_kv(kcr, vcr, kpos, kw1, kb1, kw2, vpos, vw1, vb1, vw2)
    n_sel = T // SEL_BLOCK
    overlap = cmp_to_sel(kc.shape[1], n_sel)
    ks_b = ks.reshape(B, n_sel, SEL_BLOCK, NSA_KV, NSA_HD)
    vs_b = vs.reshape(B, n_sel, SEL_BLOCK, NSA_KV, NSA_HD)
    b_idx = jnp.arange(B)[:, None, None, None]
    g_idx = jnp.arange(NSA_KV)[None, None, :, None]

    def fetch(idx):
        return ks_b[b_idx, idx, :, g_idx], vs_b[b_idx, idx, :, g_idx]

    pad = jnp.zeros((B, WINDOW, NSA_KV, NSA_HD), kw.dtype)
    kw_p = jnp.concatenate([pad, kw], axis=1)
    vw_p = jnp.concatenate([pad, vw], axis=1)

    def block(i):
        s = i * Q_BLOCK
        qb = lax.dynamic_slice_in_dim(q, s, Q_BLOCK, axis=1)
        gb = lax.dynamic_slice_in_dim(gates, s, Q_BLOCK, axis=1)
        kwb = lax.dynamic_slice_in_dim(kw_p, s, Q_BLOCK + WINDOW, axis=1)
        vwb = lax.dynamic_slice_in_dim(vw_p, s, Q_BLOCK + WINDOW, axis=1)
        qpos = s + jnp.arange(Q_BLOCK)
        kwpos = s - WINDOW + jnp.arange(Q_BLOCK + WINDOW)
        return nsa_attend(qb, qpos, gb, kc, vc, c_end, overlap, fetch, kwb, vwb, kwpos)

    o = lax.map(block, jnp.arange(T // Q_BLOCK))
    o = jnp.moveaxis(o, 0, 1).reshape(B, T, NSA_WIDTH)
    wb = min(WINDOW, T)
    return nsa_output(x, o, z, gate, w_out), kcr, vcr, ks, vs, kw[:, T - wb:], vw[:, T - wb:]

def layer_c_sample(x, c, page_table, pool_cmp_k, pool_cmp_v, pool_sel_k, pool_sel_v, win_k, win_v,
                   norm_w, ada_w, ada_b, w_in, b_gate,
                   kpos, kw1, kb1, kw2, vpos, vw1, vb1, vw2, w_out):
    B, T, _ = x.shape
    n_pages = page_table.shape[1]
    page = pool_cmp_k.shape[1]
    past = n_pages * page
    pos = past + jnp.arange(T)
    q, kcr, vcr, ks, vs, kw, vw, gates, z, gate = nsa_inputs(x, c, pos, norm_w, ada_w, ada_b, w_in, b_gate)

    def dense(pool, new):
        return jnp.concatenate([pool[page_table].reshape(B, past, NSA_KV, NSA_HD).astype(new.dtype), new], axis=1)

    kc, vc, c_end = compressed_kv(dense(pool_cmp_k, kcr), dense(pool_cmp_v, vcr), kpos, kw1, kb1, kw2, vpos, vw1, vb1, vw2)
    S = past + T
    n_sel = -(-S // SEL_BLOCK)
    overlap = cmp_to_sel(kc.shape[1], n_sel)
    n_past_blk = past // SEL_BLOCK
    n_new_blk = n_sel - n_past_blk
    bpp = page // SEL_BLOCK

    def new_blocks(a):
        a = jnp.pad(a, ((0, 0), (0, n_new_blk * SEL_BLOCK - T), (0, 0), (0, 0)))
        return a.reshape(B, n_new_blk, SEL_BLOCK, NSA_KV, NSA_HD)

    ks_new, vs_new = new_blocks(ks), new_blocks(vs)
    pk = pool_sel_k.reshape(-1, bpp, SEL_BLOCK, NSA_KV, NSA_HD)
    pv = pool_sel_v.reshape(-1, bpp, SEL_BLOCK, NSA_KV, NSA_HD)
    b_idx = jnp.arange(B)[:, None, None, None]
    g_idx = jnp.arange(NSA_KV)[None, None, :, None]

    def fetch(idx):
        in_past = (idx < n_past_blk)[..., None, None]
        pg = page_table[b_idx, jnp.minimum(idx // bpp, n_pages - 1)]
        sub = idx % bpp
        j = jnp.clip(idx - n_past_blk, 0, n_new_blk - 1)

        def get(pool, new):
            return jnp.where(in_past, pool[pg, sub, :, g_idx].astype(new.dtype), new[b_idx, j, :, g_idx])

        return get(pk, ks_new), get(pv, vs_new)

    wb = win_k.shape[1]
    kw_all = jnp.concatenate([win_k.astype(kw.dtype), kw], axis=1)
    vw_all = jnp.concatenate([win_v.astype(vw.dtype), vw], axis=1)
    kw_pos = past - wb + jnp.arange(wb + T)
    o = nsa_attend(q, pos, gates, kc, vc, c_end, overlap, fetch, kw_all, vw_all, kw_pos)
    y = nsa_output(x, o.reshape(B, T, NSA_WIDTH), z, gate, w_out)
    return y, kcr, vcr, ks, vs, kw_all[:, T:], vw_all[:, T:]

def setup_inputs(seed: int = 0) -> dict:
    key = jax.random.key(seed)
    keys = iter(jax.random.split(key, 64))

    def nrm(shape, std=1.0):
        return jax.random.normal(next(keys), shape, jnp.float32) * std

    NA, NC, D = N_A_LAYERS, N_C_LAYERS, D_MODEL
    n_pages = PAST_LEN // PAGE_SIZE
    used = DEC_BATCH * n_pages
    pool_pages = used + max(1, used // 4)
    win_buf = min(WINDOW, PAST_LEN)
    page_table = jax.random.permutation(next(keys), pool_pages)[:used].reshape(DEC_BATCH, n_pages).astype(jnp.int32)
    kv_pool = (NC, pool_pages, PAGE_SIZE, NSA_KV, NSA_HD)
    f_bias = jnp.linspace(3.0, 6.0, MLSTM_HEADS, dtype=jnp.float32)
    return {
        "x_prompt": nrm((BATCH, SEQ, D)),
        "x_sample": nrm((DEC_BATCH, DEC_SEQ, D)),
        "c_prompt": nrm((BATCH, D)),
        "c_sample": nrm((DEC_BATCH, D)),
        "state_pool": nrm((NA, DEC_BATCH, POOL_BUF, POOL_WIDTH)),
        "state_conv": nrm((NA, DEC_BATCH, CONV_W - 1, 2 * MLSTM_WIDTH)),
        "state_C": nrm((NA, DEC_BATCH, MLSTM_HEADS, MLSTM_HD, MLSTM_HD), 0.1),
        "state_n": nrm((NA, DEC_BATCH, MLSTM_HEADS, MLSTM_HD), 0.1),
        "state_m": nrm((NA, DEC_BATCH, MLSTM_HEADS), 0.5),
        "cache_cmp_k": nrm(kv_pool),
        "cache_cmp_v": nrm(kv_pool),
        "cache_sel_k": nrm(kv_pool),
        "cache_sel_v": nrm(kv_pool),
        "cache_win_k": nrm((NC, DEC_BATCH, win_buf, NSA_KV, NSA_HD)),
        "cache_win_v": nrm((NC, DEC_BATCH, win_buf, NSA_KV, NSA_HD)),
        "page_table": page_table,
        "a_norm": 1.0 + nrm((NA, D), 0.02),
        "a_ada_w": nrm((NA, D, 3 * D), 0.5 * D ** -0.5),
        "a_ada_b": nrm((NA, 3 * D), 0.02),
        "a_w_in": nrm((NA, D, IN_A), D ** -0.5),
        "a_b_if": jnp.concatenate([nrm((NA, MLSTM_HEADS), 0.1), f_bias + nrm((NA, MLSTM_HEADS), 0.1)], axis=-1),
        "a_pool_w": nrm((NA, POOL_GROUPS, POOL_GW, POOL_GW), POOL_GW ** -0.5),
        "a_pool_scale": 1.0 + nrm((NA, POOL_WIDTH), 0.1),
        "a_conv_w": nrm((NA, CONV_W, 2 * MLSTM_WIDTH), CONV_W ** -0.5),
        "a_conv_b": nrm((NA, 2 * MLSTM_WIDTH), 0.02),
        "a_head_norm": 1.0 + nrm((NA, MLSTM_WIDTH), 0.02),
        "a_w_out": nrm((NA, MIX_A, D), MIX_A ** -0.5),
        "c_norm": 1.0 + nrm((NC, D), 0.02),
        "c_ada_w": nrm((NC, D, 3 * D), 0.5 * D ** -0.5),
        "c_ada_b": nrm((NC, 3 * D), 0.02),
        "c_w_in": nrm((NC, D, IN_C), D ** -0.5),
        "c_b_gate": nrm((NC, 3 * NSA_HEADS), 0.1),
        "c_cmp_k_pos": CMP_BLOCK ** -0.5 * (1.0 + nrm((NC, CMP_BLOCK), 0.1)),
        "c_cmp_k_w1": nrm((NC, NSA_HD, NSA_HD), NSA_HD ** -0.5),
        "c_cmp_k_b1": nrm((NC, NSA_HD), 0.02),
        "c_cmp_k_w2": nrm((NC, NSA_HD, NSA_HD), 2.0 * NSA_HD ** -0.5),
        "c_cmp_v_pos": CMP_BLOCK ** -0.5 * (1.0 + nrm((NC, CMP_BLOCK), 0.1)),
        "c_cmp_v_w1": nrm((NC, NSA_HD, NSA_HD), NSA_HD ** -0.5),
        "c_cmp_v_b1": nrm((NC, NSA_HD), 0.02),
        "c_cmp_v_w2": nrm((NC, NSA_HD, NSA_HD), 2.0 * NSA_HD ** -0.5),
        "c_w_out": nrm((NC, NSA_WIDTH, D), NSA_WIDTH ** -0.5),
        "final_norm": 1.0 + nrm((D,), 0.02),
    }

def reference(x_prompt, x_sample, c_prompt, c_sample,
              state_pool, state_conv, state_C, state_n, state_m,
              cache_cmp_k, cache_cmp_v, cache_sel_k, cache_sel_v, cache_win_k, cache_win_v,
              page_table,
              a_norm, a_ada_w, a_ada_b, a_w_in, a_b_if, a_pool_w, a_pool_scale, a_conv_w, a_conv_b, a_head_norm, a_w_out,
              c_norm, c_ada_w, c_ada_b, c_w_in, c_b_gate,
              c_cmp_k_pos, c_cmp_k_w1, c_cmp_k_b1, c_cmp_k_w2, c_cmp_v_pos, c_cmp_v_w1, c_cmp_v_b1, c_cmp_v_w2,
              c_w_out, final_norm):
    Bp = x_prompt.shape[0]
    past = page_table.shape[1] * cache_cmp_k.shape[2]
    xp, xs = x_prompt, x_sample
    pool_p, pool_s, conv_p, conv_s, C_p, C_s, n_p, n_s, m_p, m_s = ([] for _ in range(10))
    ck_p, ck_s, cv_p, cv_s, sk_p, sk_s, sv_p, sv_s, wk_p, wk_s, wv_p, wv_s = ([] for _ in range(12))
    for layer in range(DEPTH):
        i = layer // 2
        if layer % 2 == 0:
            w = (a_norm[i], a_ada_w[i], a_ada_b[i], a_w_in[i], a_b_if[i], a_pool_w[i], a_pool_scale[i],
                 a_conv_w[i], a_conv_b[i], a_head_norm[i], a_w_out[i])
            xp, pb, cb, C, n, m = layer_a(
                xp, c_prompt, 0,
                jnp.zeros((Bp, POOL_BUF, POOL_WIDTH), xp.dtype),
                jnp.zeros((Bp, CONV_W - 1, 2 * MLSTM_WIDTH), xp.dtype),
                jnp.zeros((Bp, MLSTM_HEADS, MLSTM_HD, MLSTM_HD), jnp.float32),
                jnp.zeros((Bp, MLSTM_HEADS, MLSTM_HD), jnp.float32),
                jnp.zeros((Bp, MLSTM_HEADS), jnp.float32), *w)
            pool_p.append(pb); conv_p.append(cb); C_p.append(C); n_p.append(n); m_p.append(m)
            xs, pb, cb, C, n, m = layer_a(xs, c_sample, past, state_pool[i], state_conv[i],
                                          state_C[i], state_n[i], state_m[i], *w)
            pool_s.append(pb); conv_s.append(cb); C_s.append(C); n_s.append(n); m_s.append(m)
        else:
            w = (c_norm[i], c_ada_w[i], c_ada_b[i], c_w_in[i], c_b_gate[i],
                 c_cmp_k_pos[i], c_cmp_k_w1[i], c_cmp_k_b1[i], c_cmp_k_w2[i],
                 c_cmp_v_pos[i], c_cmp_v_w1[i], c_cmp_v_b1[i], c_cmp_v_w2[i], c_w_out[i])
            xp, a1, a2, a3, a4, a5, a6 = layer_c_prompt(xp, c_prompt, *w)
            ck_p.append(a1); cv_p.append(a2); sk_p.append(a3); sv_p.append(a4); wk_p.append(a5); wv_p.append(a6)
            xs, a1, a2, a3, a4, a5, a6 = layer_c_sample(xs, c_sample, page_table, cache_cmp_k[i], cache_cmp_v[i],
                                                        cache_sel_k[i], cache_sel_v[i], cache_win_k[i], cache_win_v[i], *w)
            ck_s.append(a1); cv_s.append(a2); sk_s.append(a3); sv_s.append(a4); wk_s.append(a5); wv_s.append(a6)
    y_prompt = rmsnorm(xp, final_norm)
    y_sample = rmsnorm(xs, final_norm)
    return (y_prompt, y_sample,
            jnp.stack(pool_p), jnp.stack(pool_s), jnp.stack(conv_p), jnp.stack(conv_s),
            jnp.stack(C_p), jnp.stack(C_s), jnp.stack(n_p), jnp.stack(n_s), jnp.stack(m_p), jnp.stack(m_s),
            jnp.stack(ck_p), jnp.stack(ck_s), jnp.stack(cv_p), jnp.stack(cv_s),
            jnp.stack(sk_p), jnp.stack(sk_s), jnp.stack(sv_p), jnp.stack(sv_s),
            jnp.stack(wk_p), jnp.stack(wk_s), jnp.stack(wv_p), jnp.stack(wv_s))


_drawn_inputs = setup_inputs


def setup_inputs(seed=0):
    import zlib

    import numpy as np

    out = dict(_drawn_inputs(seed))
    spreads = {}
    factors = {'cache_cmp_k': 2.832,
     'cache_sel_k': 8.0,
     'cache_sel_v': 8.0,
     'a_pool_scale': 4.346,
     'a_head_norm': 8.0,
     'c_norm': 2.803,
     'c_b_gate': 6.893,
     'c_cmp_k_pos': 8.0,
     'c_cmp_k_b1': 8.0,
     'c_cmp_v_pos': 5.847,
     'c_cmp_v_b1': 22.642,
     'final_norm': 7.724}
    for name, (base, spread) in spreads.items():
        noise = np.random.default_rng([zlib.crc32(name.encode()), seed]).standard_normal(out[name].shape)
        drawn = base * np.exp(spread * noise) if base else spread * noise
        out[name] = __import__('jax').numpy.asarray(drawn.astype(out[name].dtype))
    for name, factor in factors.items():
        out[name] = (out[name] * factor).astype(out[name].dtype)
    return out
```

```python
from contextlib import ExitStack

import numpy as np
import concourse.bass as bass
from concourse import mybir

F32 = mybir.dt.float32
I32 = mybir.dt.int32
ALU = mybir.AluOpType
ACT = mybir.ActivationFunctionType
AX = mybir.AxisListType

P = 128
D = 1024
KT = D // P
TP = 512
NB = 8
TS = 8
NS = NB * TS
NT = TP + NS
PT_TILES = TP // P
H = 4
HD = 128
G = 4
R = 4
KVW = 256
DH = 64
PAGES = 32
PAST = PAGES * P
NSEL = 65
NCMP = 255
NCMP_P = 31
NEG = -1e30
EPS = 1e-6
TINY = 2.0 ** -126
POOL_W = (2, 4, 8, 16)
PL = 15 + TP
PS = 15 + TS
CL = 3 + TP
CS = 3 + TS
RING = 3
CHUNK = 512

CONST = {}


def const_array():
    parts, at = [], 0

    def put(name, a):
        nonlocal at
        full = np.zeros((P, a.shape[1]), np.float32)
        full[:a.shape[0]] = a
        CONST[name] = (at, a.shape[1])
        parts.append(full)
        at += a.shape[1]

    i = np.arange(P)



    put("causal_keep", (i[:, None] <= i[None, :]).astype(float))
    s = np.arange(NS)
    put("block_keep", ((s[:, None] // TS == s[None, :] // TS) & (s[:, None] <= s[None, :])).astype(float))
    put("batch_rows", (s[:, None] // TS == np.arange(NB)[None, :]).astype(float))
    put("head_rows", np.repeat(np.eye(H), P, axis=1))
    seg = np.ones(NT)
    seg[0] = 0
    seg[TP::TS] = 0
    put("seg_keep", np.tile(seg, (H, 1)))
    put("seg_cut", np.tile(np.where(seg == 0, NEG, 0.0), (H, 1)))
    cnt = np.minimum(np.arange(16)[None, :] + 1, np.array(POOL_W)[:, None])
    put("first_counts", np.tile((1.0 / cnt).reshape(1, -1), (P, 1)))
    half = DH // 8
    freq = np.power(np.float32(500000.0), -2.0 * np.arange(half, dtype=np.float32) / 16).astype(np.float32)

    def rope(pos):
        ang = pos.astype(np.float32)[None, :] * freq[:, None]
        c, sn = np.cos(ang.astype(np.float64)), np.sin(ang.astype(np.float64))
        n = pos.size
        cos, sin = np.ones((DH, n)), np.zeros((DH, n))
        cos[0:8], cos[8:16] = c, c
        sin[0:8], sin[8:16] = -sn, sn
        return np.tile(cos, (2, 1)), np.tile(sin, (2, 1))

    tok = np.concatenate([np.arange(TP), PAST + np.tile(np.arange(TS), NB)])
    c, sn = rope(tok)
    put("tok_cos", c)
    put("tok_sin", sn)
    swap = np.zeros((P, P))
    for g in range(2):
        for d in range(8):
            swap[g * DH + d + 8, g * DH + d] = 1
            swap[g * DH + d, g * DH + d + 8] = 1
    put("swap", swap)
    put("causal_add", np.where(i[None, :] <= i[:, None], 0.0, NEG))
    q = np.arange(TP).reshape(PT_TILES, P).T[:, :, None]
    ok = (np.arange(NCMP_P) * 16 + 31)[None, None, :] <= q
    put("pcmp_add", np.where(ok, 0.0, NEG).reshape(P, -1))
    put("pcmp_keep", ok.astype(float).reshape(P, -1))
    put("sub_rows", (i[:, None] // 16 == np.arange(8)[None, :]).astype(float))
    rows_t = (i % 32) // R
    put("row_token", np.stack([(s[:, None] == b * TS + rows_t[None, :]) for b in range(NB)], 1).reshape(NS, -1).astype(float))
    put("row_head", np.repeat(((i // 32) * R + i % R)[:, None] == np.arange(16)[None, :], 3, axis=1).astype(float))
    CONST["second part"] = at
    c, sn = rope(np.arange(NCMP) * 16 + 31)
    put("cmp_cos", c)
    put("cmp_sin", sn)
    kpos = PAST - TP + np.arange(TP)
    put("win_add", np.where(kpos[None, :] > PAST + rows_t[:, None] - TP, 0.0, NEG))
    new = np.stack([np.where((s[None, :] // TS == b) & (s[None, :] % TS <= rows_t[:, None]), 0.0, NEG)
                    for b in range(NB)], 1)
    put("new_add", new.reshape(P, NB * NS))
    put("rep_sum", (i[:, None] // R == i[None, :] // R).astype(float))
    n = np.arange(2 * P)
    ss = np.arange(NSEL) * 64
    ov = (n[:, None] * 16 < ss[None, :] + 64) & (n[:, None] * 16 + 32 > ss[None, :])
    ov[NCMP:] = False
    put("overlap", ov.reshape(2, P, NSEL).transpose(1, 0, 2).reshape(P, -1).astype(float))
    force = np.zeros(NSEL)
    force[[0, NSEL - 1, NSEL - 2]] = 1e4
    put("force", np.tile(force, (P, 1)))
    return np.concatenate(parts, axis=1).astype(np.float32)


SMALL = {}


def small_array(v):
    parts, at = [], 0

    def put(name, a):
        nonlocal at
        a = np.asarray(a).reshape(a.shape[0], -1)
        full = np.zeros((P, a.shape[1]), np.float32)
        full[:a.shape[0]] = a
        SMALL[name] = (at, a.shape[1])
        parts.append(full)
        at += a.shape[1]

    def cols(a):
        return a.reshape(-1, P).T

    c = np.concatenate([v["c_prompt"], v["c_sample"]], axis=0)
    put("c", c.T.reshape(KT, P, 1 + NB).transpose(1, 0, 2))
    for x in "ac":
        put(x + "_norm", cols(v[x + "_norm"][0]))
        put(x + "_ada_b", cols(v[x + "_ada_b"][0]))
    put("final_norm", cols(v["final_norm"]))
    put("pool_scale", cols(v["a_pool_scale"][0]))
    put("conv_w", v["a_conv_w"][0].reshape(4, KT, P).transpose(2, 1, 0))
    put("conv_b", cols(v["a_conv_b"][0]))
    put("head_norm", cols(v["a_head_norm"][0]))
    put("b_i", v["a_b_if"][0][:H].reshape(H, 1))
    put("b_f", v["a_b_if"][0][H:].reshape(H, 1))
    put("m0", v["state_m"][0].T)
    put("n0", v["state_n"][0].transpose(2, 0, 1))
    put("conv0", v["state_conv"][0].reshape(NB, 3, KT, P).transpose(3, 2, 0, 1))
    put("pool0", v["state_pool"][0].reshape(NB, 15, 4, P).transpose(3, 2, 0, 1))
    put("b_gate", np.tile(v["c_b_gate"][0].reshape(1, -1), (P, 1)))
    for x in "kv":
        put("b1" + x, np.tile(v[f"c_cmp_{x}_b1"][0], 2).reshape(P, 1))
        pos = v[f"c_cmp_{x}_pos"][0]
        put("pos" + x, np.stack([np.tile(pos[:16], 8), np.tile(pos[16:], 8)], 1))
        put("w1" + x, np.tile(v[f"c_cmp_{x}_w1"][0], (2, 1)))
        put("w2" + x, np.tile(v[f"c_cmp_{x}_w2"][0], (2, 1)))
    return np.concatenate(parts, axis=1)


def kv_columns(a, o, width=256):
    return a[:, o:o + width]


def head_pairs(w):
    k = w.shape[0]
    return w.reshape(k, 2, 2, R, DH).transpose(0, 1, 3, 2, 4).reshape(k, -1)


def weight_chunks(v):
    a, c = v["a_w_in"][0], v["c_w_in"][0]
    o = 2 * 512
    cols = [v["a_ada_w"][0]]
    cols += [a[:, o:o + 1024], a[:, 0:1024], a[:, o + 1024:o + 2560]]
    cols += [v["a_w_out"][0], v["c_ada_w"][0]]
    kc, vc, ks, vs, kw, vw = (kv_columns(c, 1024 + 256 * n) for n in range(6))
    cols += [kc, vc, ks, kw, vs, vw, head_pairs(c[:, 0:1024]), c[:, 1024 + 1536 + 48:]]
    cols += [v["c_w_out"][0]]
    w = np.concatenate(cols, axis=1)
    n = w.shape[1] // CHUNK
    return w.reshape(KT, P, n, CHUNK).transpose(2, 1, 0, 3).reshape(n, P, KT * CHUNK)


def narrow_weights(v):
    w = np.concatenate([v["a_w_in"][0][:, -8:], v["c_w_in"][0][:, 1024 + 1536:1024 + 1536 + 48]], axis=1)
    return w.reshape(KT, P, 56).transpose(1, 0, 2)


W_ADA_A, W_QK, W_POOL, W_V, W_O, W_Z, W_OUT_A = 0, 6, 8, 10, 11, 12, 13
W_ADA_C, W_CC, W_KK, W_VV, W_Q, W_ZC, W_OUT_C, W_END = 15, 21, 22, 23, 24, 26, 28, 30


class Order:

    def __init__(self, names):
        self.names = list(names)
        self.at = {n: i + 1 for i, n in enumerate(self.names)}
        assert len(self.at) == len(self.names)
        self.given = 0

    def __getitem__(self, name):
        return self.at[name]

    def one(self, name):
        assert self.names[self.given % len(self.names)] == name, (self.names[self.given % len(self.names)], name)
        self.given += 1
        return 1

    def __len__(self):
        return len(self.names)


def build(nc, v):
    with ExitStack() as ctx:
        def sbuf(name, cols, dt=F32, parts=P):
            return ctx.enter_context(nc.sbuf_tensor(name, [parts, cols], dt))

        def sem(name):
            return ctx.enter_context(nc.semaphore(name))

        fixed = sbuf("fixed", 2 * P + 1)
        small = sbuf("small", v["small"].shape[1])
        xT_ = sbuf("xT", KT * NT)
        mods = sbuf("mods", 2 * 24 * 9)
        wring_ = sbuf("wring", RING * KT * CHUNK)
        pages = sbuf("pages", NB * PAGES, I32, 1)
        AN = (nc.sbuf_bytes_remaining // 4) & ~63
        arena = sbuf("arena", AN)
        ps = ctx.enter_context(nc.psum_tensor("ps", [P, 8, 512], F32))

        ident, ones, eps = fixed[:, 0:P], fixed[:, P:2 * P], fixed[:, 2 * P:2 * P + 1]
        xT = xT_[:, :].rearrange("p (k n) -> p k n", k=KT)
        wring = wring_[:, :].rearrange("p (s k c) -> p s k c", s=RING, k=KT)
        modA = mods[:, 0:216].rearrange("p (k b) -> p k b", b=9)
        modC = mods[:, 216:432].rearrange("p (k b) -> p k b", b=9)

        def sm(name):
            o, w = SMALL[name]
            return small[:, o:o + w]

        top = [0]

        def take(cols):
            o = top[0]
            top[0] += cols
            assert top[0] <= AN, (top[0], AN)
            return arena[:, o:o + cols]

        plan_a = [(W_ADA_A + n, "A", n) for n in range(6)]
        plan_a += [(W_QK + n // 4, "F", n) for n in range(8)]
        plan_a += [(W_POOL + n // 4, "F", n) for n in range(8)]
        plan_a += [(W_V, "T", n) for n in range(5)]
        plan_a += [(W_O, "F", n) for n in range(4)] + [(W_Z, "F", n) for n in range(4)]
        plan_a += [(None, "N", 0), (None, "N", 1)]
        plan_ao = [(W_OUT_A + n // 4, "F", n) for n in range(8)] + [(W_ADA_C + n, "A", n) for n in range(6)]
        plan_c = [(W_CC, "T", n) for n in range(5)] + [(W_KK, "F", n) for n in range(4)]
        plan_c += [(W_VV, "T", n) for n in range(5)] + [(W_Q + n // 4, "F", n) for n in range(8)]
        plan_c += [(W_ZC + n // 4, "F", n) for n in range(8)] + [(None, "N", n) for n in range(5)]
        plan_co = [(W_OUT_C + n // 4, "F", n) for n in range(8)]
        unit_end, u = {}, 0
        first_unit = {}
        for name, plan in (("a", plan_a), ("ao", plan_ao), ("c", plan_c), ("co", plan_co)):
            first_unit[name] = u
            for chunk, _, _ in plan:
                u += 1
                unit_end[chunk] = u
        proj_done, proj_evac = sem("proj_done"), sem("proj_evac")
        w_ready = [sem(f"w_ready{i}") for i in range(RING)]
        sent = [0]

        def send_weights(sp, upto):
            while sent[0] < min(upto, W_END):
                n = sent[0]
                if n >= RING:
                    sp.wait_ge(proj_done, unit_end[n - RING])
                sp.dma_start(wring_[:, (n % RING) * KT * CHUNK:(n % RING + 1) * KT * CHUNK],
                             v["weights"][n]).then_inc(w_ready[n % RING], 16)
                sent[0] += 1

        def project(pe, name, plan, moving, narrow, between=None, ready=None):
            seen = set()
            for i, (chunk, kind, index) in enumerate(plan):
                u = first_unit[name] + i
                if chunk is not None and chunk not in seen:
                    seen.add(chunk)
                    pe.wait_ge(w_ready[chunk % RING], 16 * (chunk // RING + 1))
                if ready is not None:
                    ready(i)
                if u >= 3:
                    pe.wait_ge(proj_evac, u - 2)
                main, samp = ps[:, 2 * (u % 3), :], ps[:, 2 * (u % 3) + 1, :]
                w = wring[:, chunk % RING] if chunk is not None else None
                if kind == "A":
                    silu_c = moving
                    for ct in range(4):
                        for k in range(KT):
                            last = pe.matmul(main[:, 9 * ct:9 * ct + 9], w[:, k, ct * P:ct * P + P], silu_c[:, k, :],
                                             start=(k == 0), stop=(k == KT - 1))
                elif kind == "F":
                    ct = index % 4
                    for k in range(KT):
                        pe.matmul(main[:, :], w[:, k, ct * P:ct * P + P], moving[k][:, 0:TP],
                                  start=(k == 0), stop=(k == KT - 1))
                    for k in range(KT):
                        last = pe.matmul(samp[:, 0:NS], w[:, k, ct * P:ct * P + P], moving[k][:, TP:NT],
                                         start=(k == 0), stop=(k == KT - 1))
                elif kind == "T":
                    m = P if index < 4 else NS
                    for k in range(KT):
                        last = pe.matmul(main[0:m, :], moving[k][:, index * P:index * P + m], w[:, k, :],
                                         start=(k == 0), stop=(k == KT - 1))
                elif name == "a":
                    for k in range(KT):
                        pe.matmul(main[0:H, :], narrow[:, k, H * index:H * index + H], moving[k][:, 0:TP],
                                  start=(k == 0), stop=(k == KT - 1))
                    for k in range(KT):
                        last = pe.matmul(samp[0:H, 0:NS], narrow[:, k, H * index:H * index + H], moving[k][:, TP:NT],
                                         start=(k == 0), stop=(k == KT - 1))
                else:
                    m = P if index < 4 else NS
                    for k in range(KT):
                        last = pe.matmul(main[0:m, 0:48], moving[k][:, index * P:index * P + m], narrow[:, k, 8:56],
                                         start=(k == 0), stop=(k == KT - 1))
                last.then_inc(proj_done, 1)
                if between is not None:
                    between(i)

        def banks(name, i):
            u = first_unit[name] + i
            return ps[:, 2 * (u % 3), :], ps[:, 2 * (u % 3) + 1, :]

        in_small, in_x, in_n = sem("in_small"), sem("in_x"), sem("in_n")
        constA = take(v["constA"].shape[1])
        narrow_ = take(KT * 56)
        narrow = narrow_.rearrange("p (k c) -> p k c", k=KT)

        def ca(name, parts=P):
            o, w = CONST[name]
            return constA[0:parts, o:o + w]

        qk_ = take(KT * NT)
        qk = qk_.rearrange("p (k n) -> p k n", k=KT)
        yp = take(4 * NT).rearrange("p (k n) -> p k n", k=4)
        va = take(5 * H * 129).rearrange("p (t h e) -> p t h e", t=5, h=H)
        og = take(4 * NT).rearrange("p (k n) -> p k n", k=4)
        ig, fx = take(NT), take(NT)
        csilu = take(KT * 9).rearrange("p (k b) -> p k b", k=KT)
        mark_a = top[0]
        h_ = take(KT * NT)
        hT = h_.rearrange("p (k n) -> p k n", k=KT)
        qkE = take(KT * (CL + NB * CS)).rearrange("p (k n) -> p k n", k=KT)
        xpE = take(4 * (PL + NB * PS)).rearrange("p (k n) -> p k n", k=4)
        ztmp = take(NT)
        cv = take(2 * NT).rearrange("p (s n) -> p s n", s=2)
        std = take(NT)
        pstage = take(4 * 9 * 15).rearrange("p (k b j) -> p k b j", k=4, b=9)
        cstage = take(KT * 9 * 3).rearrange("p (k b j) -> p k b j", k=KT, b=9)
        plA, plB = take(PL + NB * PS), take(PL + NB * PS)
        dbuf = take(2 * NT).rearrange("p (s n) -> p s n", s=2)
        poolw_ = take(4 * P)
        poolw = poolw_.rearrange("p (g o) -> p g o", g=4)
        amod = take(KT * 9).rearrange("p (k b) -> p k b", k=KT)

        class Norm:

            def __init__(self, name, mod, norm, h, sq, std, am):
                self.mod, self.norm, self.h, self.sq, self.std, self.am = mod, norm, h, sq, std, am
                self.squared, self.summed, self.rooted = sem(name + "_squared"), sem(name + "_summed"), sem(name + "_rooted")
                self.scaled, self.h_prompt, self.h_sample = sem(name + "_scaled"), sem(name + "_hp"), sem(name + "_hs")

        def norm_act(act, n):
            act.activation(n.sq, xT_[:, :], ACT.Square).then_inc(n.squared, 1)
            act.wait_ge(n.summed, 1)
            act.activation(n.std[:, 0:TP], ps[:, 6, :], ACT.Sqrt, scale=1.0 / D, bias=eps[:, 0:1])
            act.activation(n.std[:, TP:NT], ps[:, 7, 0:NS], ACT.Sqrt, scale=1.0 / D, bias=eps[:, 0:1]).then_inc(n.rooted, 1)

        def norm_act_prompt(act, n):
            act.wait_ge(n.scaled, 1)
            for k in range(KT):
                act.activation(n.h[:, k, 0:TP], n.h[:, k, 0:TP], ACT.Identity,
                               scale=n.am[:, k, 0:1], bias=n.mod[:, k, 0:1]).then_inc(n.h_prompt, 1)

        def norm_pe(pe, n):
            pe.wait_ge(n.squared, 1)
            sq = n.sq.rearrange("p (k n) -> p k n", k=KT)
            for k in range(KT):
                pe.matmul(ps[:, 6, :], ones, sq[:, k, 0:TP], start=(k == 0), stop=(k == KT - 1))
            for k in range(KT):
                last = pe.matmul(ps[:, 7, 0:NS], ones, sq[:, k, TP:NT], start=(k == 0), stop=(k == KT - 1))
            last.then_inc(n.summed, 1)

        def norm_dve(dve, n):
            dve.scalar_tensor_tensor(out=n.am, in0=n.mod[:, 8:16, :], scalar=1.0,
                                     in1=n.norm.unsqueeze(2).to_broadcast([P, KT, 9]), op0=ALU.add, op1=ALU.mult)
            dve.wait_ge(n.rooted, 1)
            dve.reciprocal(n.std, n.std)
            dve.drain()
            dve.tensor_tensor(n.h, xT, n.std.unsqueeze(1).to_broadcast([P, KT, NT]), ALU.mult).then_inc(n.scaled, 1)
            dve.drain()
            hs = n.h[:, :, TP:NT].rearrange("p k (b t) -> p k b t", b=NB)
            dve.tensor_tensor(hs, hs, n.am[:, :, 1:9].unsqueeze(3).to_broadcast([P, KT, NB, TS]), ALU.mult)
            dve.drain()
            dve.tensor_tensor(hs, hs, n.mod[:, 0:8, 1:9].unsqueeze(3).to_broadcast([P, KT, NB, TS]),
                              ALU.add).then_inc(n.h_sample, 1)

        nA = Norm("normA", modA, sm("a_norm"), hT, qk_, std, amod)
        csilu_done = sem("csilu_done")
        pads_done, conv_done, conv_free = sem("pads_done"), sem("conv_done"), sem("conv_free")
        pool_mm, gate_done = sem("pool_mm"), sem("gate_done")
        pool_in, pool_out, out_staged, outs = sem("pool_in"), sem("pool_out"), sem("out_staged"), sem("outs")
        n_outs = [0]

        def store(eng, dst, src):
            n_outs[0] += 16
            eng.dma_start(dst, src).then_inc(outs, 16)

        with nc.Block() as block:
            @block.sync
            def _(sp):
                sp.dma_start(small[:, :], v["small"]).then_inc(in_small, 16)
                sp.dma_start(fixed[:, :], v["fixed"]).then_inc(in_small, 16)
                sp.dma_start(constA[:, :], v["constA"]).then_inc(in_small, 16)
                send_weights(sp, 1)
                sp.dma_start(xT_[:, :], v["x"]).then_inc(in_x, 16)
                sp.dma_start(narrow_, v["narrow"]).then_inc(in_n, 16)
                sp.dma_start(poolw_, v["pool_w"]).then_inc(in_n, 16)
                sp.dma_start(pages[:, :], v["page_table"]).then_inc(in_n, 16)
                send_weights(sp, W_Z + 1 + RING)
                sp.wait_ge(out_staged, 2)
                store(sp, v["conv_out"], cstage)
                store(sp, v["pool_out"], pstage)
                sp.wait_ge(outs, n_outs[0])

            @block.gpsimd
            def _(pool):
                pool.memset(va, 1.0).then_inc(pads_done, 1)
                pool.memset(qkE[:, :, 0:3], 0.0).then_inc(pads_done, 1)
                pool.memset(xpE[:, :, 0:15], 0.0).then_inc(pads_done, 1)

            @block.tensor
            def _(pe):
                def ready(i):
                    if i == 0:
                        pe.wait_ge(csilu_done, 1)
                    if i == 1:
                        norm_pe(pe, nA)
                    if i == 6:
                        pe.wait_ge(nA.h_prompt, KT)
                        pe.wait_ge(nA.h_sample, 1)
                        pe.wait_ge(in_n, 48)

                mv = [hT[:, k, :] for k in range(KT)]
                project(pe, "a", plan_a[:6], csilu, narrow, ready=ready)
                first_unit["a"] += 6

                def pool_mix(i):
                    g = i + 6 - 19
                    if 0 <= g < 4:
                        pe.wait_ge(pool_in, g + 1)
                        if g >= 1:
                            pe.wait_ge(pool_out, g)
                        d = dbuf[:, g % 2, :]
                        pe.matmul(ps[:, 6, :], poolw[:, g, :], d[:, 0:TP], start=True, stop=True)
                        pe.matmul(ps[:, 7, 0:NS], poolw[:, g, :], d[:, TP:NT], start=True, stop=True).then_inc(pool_mm, 1)

                project(pe, "a", plan_a[6:], mv, narrow, ready=lambda i: ready(i + 6), between=pool_mix)
                first_unit["a"] -= 6

            @block.scalar
            def _(act):
                act.wait_ge(in_small, 48)
                act.activation(csilu.rearrange("p k b -> p (k b)"), sm("c"), ACT.Silu).then_inc(csilu_done, 1)
                act.wait_ge(in_x, 16)
                norm_act(act, nA)
                u0 = first_unit["a"]

                def evac_ada(i, mod, bias):
                    act.wait_ge(proj_done, u0 + i + 1)
                    main, _ = banks("a", i)
                    for ct in range(4):
                        k = 4 * i + ct
                        last = act.activation(mod[:, k, :], main[:, 9 * ct:9 * ct + 9], ACT.Identity, bias=bias[:, k:k + 1])
                    last.then_inc(proj_evac, 1)

                for i in range(6):
                    evac_ada(i, modA, sm("a_ada_b"))
                norm_act_prompt(act, nA)
                act.wait_ge(pads_done, 3)
                for i, (chunk, kind, index) in enumerate(plan_a):
                    if i < 6:
                        continue
                    main, samp = banks("a", i)
                    act.wait_ge(proj_done, u0 + i + 1)
                    s8 = samp[:, 0:NS].rearrange("p (b t) -> p b t", b=NB)
                    if chunk in (W_QK, W_QK + 1):
                        act.activation(qkE[:, index, 3:CL], main[:, :], ACT.Copy)
                        last = act.activation(qkE[:, index, CL:].rearrange("p (b j) -> p b j", b=NB)[:, :, 3:CS], s8, ACT.Copy)
                    elif chunk == W_POOL:
                        act.activation(xpE[:, index, 15:PL], main[:, :], ACT.Copy)
                        last = act.activation(xpE[:, index, PL:].rearrange("p (b j) -> p b j", b=NB)[:, :, 15:PS], s8, ACT.Copy)
                    elif chunk == W_POOL + 1:
                        act.activation(yp[:, index - 4, 0:TP], main[:, :], ACT.Silu)
                        last = act.activation(yp[:, index - 4, TP:NT], samp[:, 0:NS], ACT.Silu)
                    elif chunk == W_V:
                        m = P if index < 4 else NS
                        last = act.activation(va[0:m, index, :, 0:HD], main[0:m, :].rearrange("p (h e) -> p h e", h=H), ACT.Copy)
                    elif chunk == W_O:
                        act.activation(og[:, index, 0:TP], main[:, :], ACT.Sigmoid)
                        last = act.activation(og[:, index, TP:NT], samp[:, 0:NS], ACT.Sigmoid)
                    elif chunk == W_Z:
                        if index:
                            act.wait_ge(gate_done, index)
                        act.activation(ztmp[:, 0:TP], main[:, :], ACT.Silu)
                        last = act.activation(ztmp[:, TP:NT], samp[:, 0:NS], ACT.Silu)
                    else:
                        row, bias = (ig, sm("b_i")) if index == 0 else (fx, sm("b_f"))
                        act.activation(row[0:H, 0:TP], main[0:H, :], ACT.Identity, bias=bias[0:H, :])
                        last = act.activation(row[0:H, TP:NT], samp[0:H, 0:NS], ACT.Identity, bias=bias[0:H, :])
                    last.then_inc(proj_evac, 1)
                    j = i - 8
                    if 0 <= j < KT:
                        act.wait_ge(conv_done, j + 1)
                        act.activation(qk[:, j, :], cv[:, j % 2, :], ACT.Silu).then_inc(conv_free, 1)

            @block.vector
            def _(dve):
                u0 = first_unit["a"]
                dve.wait_ge(in_small, 48)
                dve.wait_ge(proj_evac, 6)
                norm_dve(dve, nA)
                conv0 = sm("conv0").rearrange("p (k b j) -> p k b j", k=KT, b=NB)
                pool0 = sm("pool0").rearrange("p (k b j) -> p k b j", k=4, b=NB)
                cw = sm("conv_w").rearrange("p (k j) -> p k j", k=KT)
                cb = sm("conv_b")
                dve.tensor_copy(qkE[:, :, CL:].rearrange("p k (b j) -> p k b j", b=NB)[:, :, :, 0:3], conv0)
                dve.tensor_copy(xpE[:, :, PL:].rearrange("p k (b j) -> p k b j", b=NB)[:, :, :, 0:15], pool0)
                dve.wait_ge(pads_done, 3)

                def conv(i):
                    dve.wait_ge(proj_evac, u0 + 7 + i)
                    if i >= 2:
                        dve.wait_ge(conv_free, i - 1)
                    y = cv[:, i % 2, :]
                    xp_ = qkE[:, i, 0:CL]
                    xs = qkE[:, i, CL:].rearrange("p (b j) -> p b j", b=NB)
                    ys = y[:, TP:NT].rearrange("p (b t) -> p b t", b=NB)
                    dve.drain()
                    dve.tensor_scalar(y[:, 0:TP], xp_[:, 0:TP], cw[:, i, 0:1], cb[:, i:i + 1], ALU.mult, ALU.add)
                    dve.tensor_scalar(ys, xs[:, :, 0:TS], cw[:, i, 0:1], cb[:, i:i + 1], ALU.mult, ALU.add)
                    for j in range(1, 4):
                        dve.drain()
                        dve.scalar_tensor_tensor(out=y[:, 0:TP], in0=xp_[:, j:j + TP], scalar=cw[:, i, j:j + 1],
                                                 in1=y[:, 0:TP], op0=ALU.mult, op1=ALU.add)
                        last = dve.scalar_tensor_tensor(out=ys, in0=xs[:, :, j:j + TS], scalar=cw[:, i, j:j + 1],
                                                        in1=ys, op0=ALU.mult, op1=ALU.add)
                    last.then_inc(conv_done, 1)

                for i in range(KT):
                    conv(i)
                first = ca("first_counts").rearrange("p (g t) -> p g t", g=4)

                def pool(g):
                    w = POOL_W[g]
                    dve.wait_ge(proj_evac, u0 + 15 + g)
                    x = xpE[:, g, :]
                    xs_ = x[:, PL:].rearrange("p (b j) -> p b j", b=NB)
                    src, step, bufs = x, 1, [plA, plB]
                    for n in range(g + 1):
                        out = bufs[n % 2]
                        dve.drain()
                        ss, os_ = src[:, PL:].rearrange("p (b j) -> p b j", b=NB), out[:, PL:].rearrange("p (b j) -> p b j", b=NB)
                        lo = 2 * step - 1
                        dve.tensor_tensor(out[:, lo:PL], src[:, lo:PL], src[:, lo - step:PL - step], ALU.add)
                        dve.tensor_tensor(os_[:, :, lo:], ss[:, :, lo:], ss[:, :, lo - step:PS - step], ALU.add)
                        src, step = out, 2 * step
                    dve.drain()
                    if g >= 2:
                        dve.wait_ge(pool_mm, g - 1)
                    d = dbuf[:, g % 2, :]
                    dve.tensor_tensor(d[:, 0:16], src[:, 15:31], first[:, g, :], ALU.mult)
                    dve.scalar_tensor_tensor(out=d[:, 16:TP], in0=src[:, 31:PL], scalar=1.0 / w, in1=x[:, 31:PL],
                                             op0=ALU.mult, op1=ALU.subtract)
                    ds_ = d[:, TP:NT].rearrange("p (b t) -> p b t", b=NB)
                    dve.scalar_tensor_tensor(out=ds_, in0=src[:, PL:].rearrange("p (b j) -> p b j", b=NB)[:, :, 15:],
                                             scalar=1.0 / w, in1=xs_[:, :, 15:], op0=ALU.mult, op1=ALU.subtract)
                    dve.drain()
                    dve.tensor_tensor(d[:, 0:16], d[:, 0:16], x[:, 15:31], ALU.subtract).then_inc(pool_in, 1)

                def pool_gate(g):
                    dve.wait_ge(pool_mm, g + 1)
                    dve.wait_ge(proj_evac, u0 + 19 + g)
                    sc = sm("pool_scale")[:, g:g + 1]
                    dve.scalar_tensor_tensor(out=yp[:, g, 0:TP], in0=ps[:, 6, :], scalar=sc, in1=yp[:, g, 0:TP],
                                             op0=ALU.mult, op1=ALU.mult)
                    dve.scalar_tensor_tensor(out=yp[:, g, TP:NT], in0=ps[:, 7, 0:NS], scalar=sc, in1=yp[:, g, TP:NT],
                                             op0=ALU.mult, op1=ALU.mult).then_inc(pool_out, 1)

                pool(0)
                pool(1)
                for g in range(2, 4):
                    pool_gate(g - 2)
                    pool(g)
                pool_gate(2)
                pool_gate(3)
                dve.tensor_copy(cstage[:, :, 0, :], qkE[:, :, TP:CL])
                dve.tensor_copy(cstage[:, :, 1:9, :], qkE[:, :, CL:].rearrange("p k (b j) -> p k b j", b=NB)[:, :, :, TS:CS]).then_inc(out_staged, 1)
                dve.tensor_copy(pstage[:, :, 0, :], xpE[:, :, TP:PL])
                dve.tensor_copy(pstage[:, :, 1:9, :], xpE[:, :, PL:].rearrange("p k (b j) -> p k b j", b=NB)[:, :, :, TS:PS]).then_inc(out_staged, 1)
                for i in range(4):
                    dve.wait_ge(proj_evac, u0 + 6 + 8 + 8 + 5 + 4 + i + 1)
                    dve.tensor_tensor(og[:, i, :], og[:, i, :], ztmp, ALU.mult).then_inc(gate_done, 1)

        top[0] = mark_a
        caug_ = take(NB * H * 129)
        caug = caug_.rearrange("p (b h e) -> p b h e", b=NB, h=H)
        wgk = take(5 * H * HD).rearrange("p (t h d) -> p t h d", t=5, h=H)
        hm_ = take(5 * H * HD)
        hm = hm_.rearrange("p (t h d) -> p t h d", t=5, h=H)
        den = take(5 * H)
        ssq = take(5 * H)
        t0, t1, bcum, Mrow = take(NT)[0:H], take(NT)[0:H], take(NT)[0:H], take(NT)[0:H]
        wi = take(NS)[0:H]
        mst = take(9)[0:H]
        stat_in = take(NT)
        stats_ = take(5 * P)
        stats = stats_.rearrange("p (t c) -> p t c", t=5)
        pt_at = [0, 512, 896, 1152, 1280]
        PTm = take(1280 + NS)
        eb = take(2 * TP).rearrange("p (s n) -> p s n", s=2)
        qz = take(NB * NS)
        dec = take(2 * NB).rearrange("p (s b) -> p s b", s=2)
        wgkz = take(NB * HD).rearrange("p (b d) -> p b d", b=NB)
        cst = take(H * 129).rearrange("p (h e) -> p h e", h=H)
        nst = take(9 * H)
        KS = HD ** -0.5
        in_c, zeroed = sem("in_c"), sem("zeroed")
        pe_m, act_m, dve_m = sem("pe_mlstm"), sem("act_mlstm"), sem("dve_mlstm")
        hs4 = range(H)
        PE = Order(["stats"] + [("kt", h) for h in hs4] + [n for h in hs4 for n in
                   [("bc", h)] + [("s", h, i) for i in range(5)] + [("pv", h, i) for i in range(5)] + [("cp", h)]
                   + [("cs", h, i) for i in range(3)]] + [("ht", h) for h in hs4])
        AC = Order(["ln", "rows"] + [n for h in hs4 for n in [("e", h, i) for i in range(5)]
                   + [("hm", h, i) for i in range(5)] + [("cp", h)]] + ["root"])
        DV = Order(["abs", "rows", "stats"] + [("wgk", h) for h in hs4] + [n for h in hs4 for n in
                   [("x", h, 0), ("x", h, 1), ("p", h, 0), ("x", h, 2), ("p", h, 1), ("x", h, 3), ("p", h, 2),
                    ("x", h, 4), ("p", h, 3), ("p", h, 4), ("qz", h), ("kz", h), ("cn", h, 0), ("cn", h, 1), ("cn", h, 2)]]
                   + ["staged", "squares", "hm"] + [("y", h) for h in hs4])
        head_rows = ca("head_rows", H).rearrange("p (h n) -> p h n", h=H)
        samples_of = [(0, 1, 2), (3, 4, 5), (6, 7)]
        state_bank = [7, 6, 7]

        def s_cols(st):
            return (4 - st) * P if st < 4 else NS

        with nc.Block() as block:
            @block.sync
            def _(sp):
                sp.dma_start(caug[:, :, :, 0:HD].rearrange("p b h e -> p (b h) e"), v["state_C"]).then_inc(in_c, 16)
                send_weights(sp, W_OUT_A + RING)
                sp.wait_ge(dve_m, DV["staged"])
                sp.wait_ge(act_m, AC[("cp", H - 1)])
                store(sp, v["C_s"], caug[:, :, :, 0:HD].rearrange("p b h e -> p (b h) e"))
                store(sp, v["C_p"], cst[:, :, 0:HD])
                store(sp, v["n_out"], nst)
                store(sp, v["m_out"], mst)
                sp.wait_ge(outs, n_outs[0])

            @block.gpsimd
            def _(pool):
                pool.memset(stat_in, 0.0)
                pool.memset(stats_, 1.0)
                pool.memset(hm_, 1.0)
                pool.memset(den, 1.0)
                pool.memset(qz, 0.0).then_inc(zeroed, 1)

            @block.tensor
            def _(pe):
                pe.wait_ge(act_m, AC["rows"])
                pe.wait_ge(dve_m, DV["rows"])
                for t in range(4):
                    pe.transpose(ps[:, 0, t * P:t * P + P], stat_in[:, t * P:t * P + P], ident)
                pe.transpose(ps[0:NS, 1, 0:P], stat_in[:, TP:NT], ident).then_inc(pe_m, PE.one("stats"))
                for h in hs4:
                    if h:
                        pe.wait_ge(dve_m, DV[("wgk", h - 1)])
                    for t in range(4):
                        pe.transpose(ps[:, 6, t * P:t * P + P], qk[:, 4 + h, t * P:t * P + P], ident)
                    pe.transpose(ps[0:NS, 7, 0:P], qk[:, 4 + h, TP:NT], ident).then_inc(pe_m, PE.one(("kt", h)))
                for h in hs4:
                    pe.wait_ge(dve_m, DV[("qz", h - 1)] if h else DV["stats"])
                    pe.matmul(ps[:, 0, :], head_rows[:, h, :], Mrow[:, 0:TP], start=True, stop=True)
                    pe.matmul(ps[:, 1, 0:NS], head_rows[:, h, :], Mrow[:, TP:NT], start=True, stop=True)
                    pe.matmul(ps[:, 1, NS:2 * NS], head_rows[:, h, :], wi, start=True, stop=True)
                    pe.matmul(ps[:, 1, P:P + NB], head_rows[:, h, :], wi[:, TS - 1:NS:TS], start=True, stop=True)\
                        .then_inc(pe_m, PE.one(("bc", h)))
                    for st in range(5):
                        if h or st >= 2:
                            pe.wait_ge(dve_m, DV[("p", h, st - 2)] if st >= 2 else DV[("p", h - 1, 4)])
                        lo, hi = (st * P, TP) if st < 4 else (TP, NT)
                        m = P if st < 4 else NS
                        pe.matmul(ps[0:m, 2 + st % 2, 0:hi - lo], qk[:, 4 + h, lo:lo + m], qk[:, h, lo:hi],
                                  start=True, stop=True).then_inc(pe_m, PE.one(("s", h, st)))
                    for tt in range(5):
                        if h or tt >= 2:
                            pe.wait_ge(act_m, AC[("hm", h, tt - 2)] if tt >= 2 else AC[("hm", h - 1, 4)])
                        out = ps[0:P if tt < 4 else NS, 4 + tt % 2, 0:129]
                        pe.wait_ge(dve_m, DV[("p", h, tt)])
                        if tt < 4:
                            for st in range(tt + 1):
                                o = pt_at[st] + (tt - st) * P
                                last = pe.matmul(out, PTm[:, o:o + P], va[:, st, h, :], start=(st == 0), stop=(st == tt))
                        else:
                            pe.wait_ge(dve_m, DV[("qz", h)])
                            pe.wait_ge(in_c, 16)
                            pe.matmul(out, PTm[0:NS, 1280:1280 + NS], va[0:NS, 4, h, :], start=True, stop=False)
                            for b in range(NB):
                                last = pe.matmul(out, qz[:, b * NS:b * NS + NS], caug[:, b, h, :], start=False, stop=(b == NB - 1))
                        last.then_inc(pe_m, PE.one(("pv", h, tt)))
                    pe.wait_ge(dve_m, DV[("cn", h - 1, 1)] if h else DV[("wgk", H - 1)])
                    for st in range(4):
                        last = pe.matmul(ps[:, 6, 0:129], wgk[:, st, h, :], va[:, st, h, :], start=(st == 0), stop=(st == 3))
                    last.then_inc(pe_m, PE.one(("cp", h)))
                    pe.wait_ge(dve_m, DV[("kz", h)])
                    for q, bs in enumerate(samples_of):
                        if q == 0 and h:
                            pe.wait_ge(dve_m, DV[("cn", h - 1, 2)])
                        if q == 1:
                            pe.wait_ge(act_m, AC[("cp", h)])
                        if q == 2:
                            pe.wait_ge(dve_m, DV[("cn", h, 0)])
                        for n, b in enumerate(bs):
                            last = pe.matmul(ps[:, state_bank[q], n * 129:n * 129 + 129], wgkz[0:NS, b, :], va[0:NS, 4, h, :],
                                             start=True, stop=True)
                        last.then_inc(pe_m, PE.one(("cs", h, q)))
                pe.wait_ge(dve_m, DV["hm"])
                for h in hs4:
                    for t in range(4):
                        pe.transpose(ps[:, 2 * h, t * P:t * P + P], hm[:, t, h, :], ident)
                    pe.transpose(ps[:, 2 * h + 1, 0:NS], hm[0:NS, 4, h, :], ident[0:NS, 0:NS]).then_inc(pe_m, PE.one(("ht", h)))

            @block.scalar
            def _(act):
                act.wait_ge(dve_m, DV["abs"])
                act.activation(t0, t0, ACT.Exp, scale=-1.0)
                act.drain()
                act.activation(t0, t0, ACT.Ln, bias=ones[0:H, 0:1]).then_inc(act_m, AC.one("ln"))
                act.wait_ge(dve_m, DV["rows"])
                act.activation(stat_in[32:32 + H, :], t1, ACT.Exp, scale=-1.0)
                act.activation(stat_in[64:64 + H, :], stat_in[64:64 + H, :], ACT.Exp)
                act.activation(wi, wi, ACT.Exp).then_inc(act_m, AC.one("rows"))
                for h in hs4:
                    for st in range(5):
                        m, n = (P if st < 4 else NS), s_cols(st)
                        act.wait_ge(dve_m, DV[("x", h, st)])
                        act.activation(eb[0:m, st % 2, 0:n], eb[0:m, st % 2, 0:n], ACT.Exp, scale=-1.0)\
                            .then_inc(act_m, AC.one(("e", h, st)))
                    for tt in range(5):
                        m = P if tt < 4 else NS
                        act.wait_ge(pe_m, PE[("pv", h, tt)])
                        act.activation(hm[0:m, tt, h, :], ps[0:m, 4 + tt % 2, 0:HD], ACT.Copy)
                        act.activation(den[0:m, tt * H + h:tt * H + h + 1], ps[0:m, 4 + tt % 2, HD:HD + 1], ACT.Copy)\
                            .then_inc(act_m, AC.one(("hm", h, tt)))
                    act.wait_ge(pe_m, PE[("cp", h)])
                    act.activation(cst[:, h, :], ps[:, 6, 0:129], ACT.Copy).then_inc(act_m, AC.one(("cp", h)))
                act.wait_ge(dve_m, DV["squares"])
                act.activation(ssq, ssq, ACT.Sqrt, scale=1.0 / HD, bias=eps[:, 0:1]).then_inc(act_m, AC.one("root"))

            @block.vector
            def _(dve):
                m0 = sm("m0")[0:H, :]
                dve.scalar_tensor_tensor(out=t0, in0=fx[0:H, :], scalar=-1.0, in1=fx[0:H, :], op0=ALU.mult, op1=ALU.max).then_inc(dve_m, DV.one("abs"))
                dve.wait_ge(zeroed, 1)
                dve.wait_ge(in_c, 16)
                dve.tensor_copy(caug[:, :, :, HD], sm("n0").rearrange("p (b h) -> p b h", b=NB))
                dve.wait_ge(act_m, AC["ln"])
                dve.scalar_tensor_tensor(out=t1, in0=fx[0:H, :], scalar=0.0, in1=t0, op0=ALU.min, op1=ALU.subtract)
                dve.drain()
                dve.tensor_tensor_scan(bcum, ca("seg_keep", H), t1, 0.0, ALU.mult, ALU.add)
                dve.drain()
                r = stat_in[0:H, :]
                dve.tensor_tensor(r, ig[0:H, :], bcum, ALU.subtract)
                dve.drain()
                dve.tensor_copy(t0, r)
                dve.drain()
                dve.tensor_scalar(t0[:, 0:1], t0[:, 0:1], 0.0, None, ALU.max)
                dve.tensor_tensor(t0[:, TP:NT:TS], t0[:, TP:NT:TS], m0, ALU.max)
                dve.drain()
                dve.tensor_tensor_scan(Mrow, ca("seg_cut", H), t0, NEG, ALU.add, ALU.max)
                dve.drain()
                dve.tensor_tensor(t1, bcum, Mrow, ALU.add)
                by_b = "p (b t) -> p b t"
                m_last = Mrow[:, TP + TS - 1:NT:TS].unsqueeze(2).to_broadcast([H, NB, TS])
                dve.tensor_scalar(stat_in[64:64 + H, 0:TP], r[:, 0:TP], Mrow[:, TP - 1:TP], None, ALU.subtract)
                dve.tensor_tensor(stat_in[64:64 + H, TP:NT].rearrange(by_b, b=NB), r[:, TP:NT].rearrange(by_b, b=NB), m_last, ALU.subtract)
                dve.tensor_tensor(wi.rearrange(by_b, b=NB), m0.unsqueeze(2).to_broadcast([H, NB, TS]),
                                  Mrow[:, TP:NT].rearrange(by_b, b=NB), ALU.subtract)
                dve.drain()
                dve.tensor_copy(mst[:, 0:1], t1[:, TP - 1:TP])
                dve.tensor_copy(mst[:, 1:9], t1[:, TP + TS - 1:NT:TS]).then_inc(dve_m, DV.one("rows"))
                dve.wait_ge(pe_m, PE["stats"])
                dve.tensor_copy(stats[:, 0:4, :], ps[:, 0, :].rearrange("p (t c) -> p t c", t=4))
                dve.tensor_copy(stats[0:NS, 4, :], ps[0:NS, 1, 0:P]).then_inc(dve_m, DV.one("stats"))
                dve.drain()
                for h in hs4:
                    dve.wait_ge(pe_m, PE[("kt", h)])
                    for t in range(4):
                        dve.tensor_scalar(wgk[:, t, h, :], ps[:, 6, t * P:t * P + P], stats[:, t, 64 + h:65 + h], KS, ALU.mult, ALU.mult)
                    dve.tensor_scalar(wgk[0:NS, 4, h, :], ps[0:NS, 7, 0:P], stats[0:NS, 4, 64 + h:65 + h], KS, ALU.mult, ALU.mult)\
                        .then_inc(dve_m, DV.one(("wgk", h)))

                def exponent(h, st):
                    m, n = (P if st < 4 else NS), s_cols(st)
                    mb = ps[:, 0, st * P:TP] if st < 4 else ps[0:NS, 1, 0:NS]
                    if st == 0:
                        dve.wait_ge(pe_m, PE[("bc", h)])
                    dve.drain()
                    dve.tensor_scalar(eb[0:m, st % 2, 0:n], mb, stats[0:m, st, h:h + 1], 0.0, ALU.subtract, ALU.max)\
                        .then_inc(dve_m, DV.one(("x", h, st)))

                def weights(h, st):
                    m, n = (P if st < 4 else NS), s_cols(st)
                    e = eb[0:m, st % 2, :]
                    dve.wait_ge(act_m, AC[("e", h, st)])
                    keep = ca("causal_keep") if st < 4 else ca("block_keep", NS)
                    dve.tensor_tensor(e[:, 0:m], e[:, 0:m], keep, ALU.mult)
                    dve.drain()
                    dve.wait_ge(pe_m, PE[("s", h, st)])
                    if h and st == 0:
                        dve.wait_ge(pe_m, PE[("pv", h - 1, 4)])
                    dve.scalar_tensor_tensor(out=PTm[0:m, pt_at[st]:pt_at[st] + n], in0=ps[0:m, 2 + st % 2, 0:n], scalar=KS,
                                             in1=e[:, 0:n], op0=ALU.mult, op1=ALU.mult).then_inc(dve_m, DV.one(("p", h, st)))

                for h in hs4:
                    exponent(h, 0)
                    exponent(h, 1)
                    for st in range(3):
                        weights(h, st)
                        exponent(h, st + 2)
                    weights(h, 3)
                    weights(h, 4)
                    dq = bass.AP(qz.tensor, qz.offset, [qz.ap[0], [NS + TS, NB], [1, TS]])
                    dve.tensor_tensor(dq, qk[:, h, TP:NT].rearrange("p (b t) -> p b t", b=NB),
                                      ps[:, 1, NS:2 * NS].rearrange("p (b t) -> p b t", b=NB), ALU.mult)
                    dve.tensor_copy(dec[:, h % 2, :], ps[:, 1, P:P + NB]).then_inc(dve_m, DV.one(("qz", h)))
                    if h:
                        dve.wait_ge(pe_m, PE[("cs", h - 1, 2)])
                    dve.tensor_tensor(wgkz[0:NS], wgk[0:NS, 4, h, :].unsqueeze(1).to_broadcast([NS, NB, HD]),
                                      ca("batch_rows", NS).unsqueeze(2).to_broadcast([NS, NB, HD]), ALU.mult)\
                        .then_inc(dve_m, DV.one(("kz", h)))
                    dve.wait_ge(pe_m, PE[("pv", h, 4)])
                    for q, bs in enumerate(samples_of):
                        dve.wait_ge(pe_m, PE[("cs", h, q)])
                        dve.drain()
                        for n, b in enumerate(bs):
                            last = dve.scalar_tensor_tensor(out=caug[:, b, h, :], in0=caug[:, b, h, :], scalar=dec[:, h % 2, b:b + 1],
                                                            in1=ps[:, state_bank[q], n * 129:n * 129 + 129], op0=ALU.mult, op1=ALU.add)
                        last.then_inc(dve_m, DV.one(("cn", h, q)))
                dve.drain()
                dve.wait_ge(act_m, AC[("cp", H - 1)])
                dve.tensor_copy(nst[:, 0:H], cst[:, :, HD])
                dve.tensor_copy(nst[:, H:].rearrange("p (b h) -> p b h", b=NB), caug[:, :, :, HD]).then_inc(dve_m, DV.one("staged"))
                d3 = den.rearrange("p (t h) -> p t h", t=5)
                dve.scalar_tensor_tensor(out=den, in0=den, scalar=-1.0, in1=den, op0=ALU.mult, op1=ALU.max)
                dve.drain()
                dve.tensor_tensor(d3, d3, stats[:, :, 32:32 + H], ALU.max)
                dve.drain()
                dve.reciprocal(den, den)
                dve.drain()
                hm3 = hm_.rearrange("p (t d) -> p t d", d=HD)
                sq3 = wgk.rearrange("p t h d -> p (t h) d")
                dve.tensor_tensor(hm3, hm3, den.unsqueeze(2).to_broadcast([P, 5 * H, HD]), ALU.mult)
                dve.wait_ge(pe_m, PE[("cs", H - 1, 2)])
                dve.drain()
                dve.tensor_tensor(sq3, hm3, hm3, ALU.mult)
                dve.drain()
                dve.tensor_reduce(ssq, sq3, AX.X, ALU.add).then_inc(dve_m, DV.one("squares"))
                dve.wait_ge(act_m, AC["root"])
                dve.reciprocal(ssq, ssq)
                dve.drain()
                dve.tensor_tensor(hm3, hm3, ssq.unsqueeze(2).to_broadcast([P, 5 * H, HD]), ALU.mult).then_inc(dve_m, DV.one("hm"))
                for h in hs4:
                    dve.wait_ge(pe_m, PE[("ht", h)])
                    hn = sm("head_norm")[:, h:h + 1]
                    dve.scalar_tensor_tensor(out=og[:, h, 0:TP], in0=ps[:, 2 * h, :], scalar=hn, in1=og[:, h, 0:TP],
                                             op0=ALU.mult, op1=ALU.mult)
                    dve.scalar_tensor_tensor(out=og[:, h, TP:NT], in0=ps[:, 2 * h + 1, 0:NS], scalar=hn, in1=og[:, h, TP:NT],
                                             op0=ALU.mult, op1=ALU.mult).then_inc(dve_m, DV.one(("y", h)))

        def residual(dve, name, mod, count):
            for i in range(count):
                main, samp = banks(name, i)
                dve.wait_ge(proj_done, first_unit[name] + i + 1)
                s8 = samp[:, 0:NS].rearrange("p (b t) -> p b t", b=NB)
                xs8 = xT[:, i, TP:NT].rearrange("p (b t) -> p b t", b=NB)
                dve.scalar_tensor_tensor(out=xT[:, i, 0:TP], in0=main, scalar=mod[:, 16 + i, 0:1], in1=xT[:, i, 0:TP],
                                         op0=ALU.mult, op1=ALU.add)
                dve.tensor_tensor(s8, s8, mod[:, 16 + i, 1:9].unsqueeze(2).to_broadcast([P, NB, TS]), ALU.mult)
                dve.drain()
                dve.tensor_tensor(xs8, xs8, s8, ALU.add).then_inc(proj_evac, 1)

        with nc.Block() as block:
            @block.sync
            def _(sp):
                send_weights(sp, W_ADA_C + 6 + RING)

            @block.tensor
            def _(pe):
                mv = [yp[:, k, :] for k in range(4)] + [og[:, k, :] for k in range(4)]
                project(pe, "ao", plan_ao[:8], mv, narrow)
                first_unit["ao"] += 8
                project(pe, "ao", plan_ao[8:], csilu, narrow)
                first_unit["ao"] -= 8

            @block.vector
            def _(dve):
                residual(dve, "ao", modA, 8)
                for i in range(6):
                    dve.wait_ge(proj_done, first_unit["ao"] + 8 + i + 1)
                    main, _ = banks("ao", 8 + i)
                    for ct in range(4):
                        k = 4 * i + ct
                        last = dve.tensor_scalar(modC[:, k, :], main[:, 9 * ct:9 * ct + 9], sm("c_ada_b")[:, k:k + 1], None, ALU.add)
                    last.then_inc(proj_evac, 1)

        top[0] = 0
        BASE_D = CONST["second part"]
        constD = take(v["constD"].shape[1])
        vv = take(5 * 512).rearrange("p (t c) -> p t c", t=5)
        zT = take(KT * NT).rearrange("p (k n) -> p k n", k=KT)
        qblk = take(2 * NB * P).rearrange("p (c b n) -> p c b n", c=2, b=NB)
        knew = take(4 * NS).rearrange("p (c n) -> p c n", c=4)
        wpos = take(32).rearrange("p (x l n) -> p x l n", x=2, l=2)
        w1b = take(2 * P).rearrange("p (x c) -> p x c", x=2)
        w2b = take(3 * P).rearrange("p (x c) -> p x c", x=3)
        grow = take(NB * 3).rearrange("p (b c) -> p b c", b=NB)
        mark_c = top[0]
        oP = take(4 * D).rearrange("p (t g r d) -> p t g r d", t=4, g=G, r=R)
        lohi_ = take(4 * 2 * 256)
        lohi = lohi_.rearrange("p (c l n) -> p c l n", c=4, l=2)
        pooled_, hid_ = take(4 * NCMP), take(4 * NCMP)
        pooled, hid = pooled_.rearrange("p (c n) -> p c n", c=4), hid_.rearrange("p (c n) -> p c n", c=4)
        kcT = take(2 * NCMP).rearrange("p (c n) -> p c n", c=2)
        ktmp = take(2 * NCMP).rearrange("p (c n) -> p c n", c=2)
        vcs = take(2 * KVW).rearrange("p (t c) -> p t c", t=2)
        mark_cmp = top[0]
        BASE_C = CONST["tok_cos"][0]
        constC = take(v["constC"].shape[1])
        narrow_ = hid_[:, 0:KT * 56]
        narrow = narrow_.rearrange("p (k c) -> p k c", k=KT)
        qT = take(KT * NT).rearrange("p (k n) -> p k n", k=KT)
        kk = take(4 * NT).rearrange("p (c n) -> p c n", c=4)
        gates_ = take(5 * 48)
        gates = gates_.rearrange("p (t c) -> p t c", t=5)
        ccz = take(4 * 512).rearrange("p (t c) -> p t c", t=4)
        cczs = hid_[:, KT * 56:KT * 56 + 512]
        top[0] = mark_c
        hC_ = take(KT * NT)
        hC = hC_.rearrange("p (k n) -> p k n", k=KT)
        stdC = take(NT)
        amC = take(KT * 9).rearrange("p (k b) -> p k b", k=KT)
        t2 = pooled_[:, 0:NT]

        def cc_(name, parts=P):
            o, w = CONST[name]
            return constC[0:parts, o - BASE_C:o - BASE_C + w]

        def cd(name, parts=P):
            o, w = CONST[name]
            return constD[0:parts, o - BASE_D:o - BASE_D + w]

        nC = Norm("normC", modC, sm("c_norm"), hC, zT.rearrange("p k n -> p (k n)"), stdC, amC)
        in_d, swapped, roped, set_up = sem("in_d"), sem("swapped"), sem("roped"), sem("set_up")
        gate_sum, gate_sig, qblk_done = sem("gate_sum"), sem("gate_sig"), sem("qblk_done")
        rope_unit = [5, 6, 7, 8] + list(range(14, 22))
        rope_tile = [kk[:, n, :] for n in range(4)] + [qT[:, n, :] for n in range(8)]
        u0c = first_unit["c"]

        with nc.Block() as block:
            @block.sync
            def _(sp):
                sp.dma_start(constD, v["constD"]).then_inc(in_d, 16)
                sp.dma_start(constC, v["constC"]).then_inc(in_d, 16)
                sp.dma_start(narrow_, v["narrow"]).then_inc(in_d, 16)
                send_weights(sp, W_OUT_C)
                sp.wait_ge(proj_evac, u0c + 5)
                store(sp, v["cc_p"], ccz)
                store(sp, v["cc_s"], cczs[0:NS, :])
                sp.wait_ge(proj_evac, u0c + 14)
                store(sp, v["vv_p"], vv[:, 0:4, :])
                store(sp, v["vv_s"], vv[0:NS, 4, :])
                sp.wait_ge(roped, 4)
                store(sp, v["kk"], kk)
                sp.wait_ge(outs, n_outs[0])

            @block.gpsimd
            def _(pool):
                pool.memset(gates_, 0.0)
                pool.memset(qblk, 0.0)
                pool.memset(w1b, 0.0)
                pool.memset(w2b, 0.0).then_inc(set_up, 1)

            @block.tensor
            def _(pe):
                norm_pe(pe, nC)
                pe.wait_ge(nC.h_prompt, KT)
                pe.wait_ge(nC.h_sample, 1)
                pe.wait_ge(in_d, 48)

                def swap(i):
                    if i - 1 in rope_unit:
                        n = rope_unit.index(i - 1)
                        pe.wait_ge(proj_evac, u0c + i)
                        if n:
                            pe.wait_ge(roped, n)
                        pe.matmul(ps[:, 6, :], cc_("swap"), rope_tile[n][:, 0:TP], start=True, stop=True)
                        pe.matmul(ps[:, 7, 0:NS], cc_("swap"), rope_tile[n][:, TP:NT], start=True, stop=True).then_inc(swapped, 1)

                project(pe, "c", plan_c, [hC[:, k, :] for k in range(KT)], narrow, between=swap)

            @block.scalar
            def _(act):
                norm_act(act, nC)
                norm_act_prompt(act, nC)
                act.wait_ge(set_up, 1)
                act.wait_ge(nC.summed, 1)
                for i, (chunk, kind, index) in enumerate(plan_c):
                    main, samp = banks("c", i)
                    act.wait_ge(proj_done, u0c + i + 1)
                    m = P if index < 4 else NS
                    if chunk in (W_CC, W_VV):
                        out = vv[:, index, :] if chunk == W_VV else (ccz[:, index, :] if index < 4 else cczs)
                        last = act.activation(out[0:m, :], main[0:m, :], ACT.Copy)
                    elif chunk is None:
                        last = act.activation(gates[0:m, index, :], main[0:m, 0:48], ACT.Copy)
                    else:
                        z = chunk in (W_ZC, W_ZC + 1)
                        out = kk[:, index, :] if chunk == W_KK else (zT if z else qT)[:, index, :]
                        f = ACT.Silu if z else ACT.Copy
                        act.activation(out[:, 0:TP], main[:, :], f)
                        last = act.activation(out[:, TP:NT], samp[:, 0:NS], f)
                    last.then_inc(proj_evac, 1)
                act.wait_ge(gate_sum, 1)
                act.activation(gates_, gates_, ACT.Sigmoid).then_inc(gate_sig, 1)

            @block.vector
            def _(dve):
                norm_dve(dve, nC)
                dve.wait_ge(in_d, 48)
                dve.wait_ge(set_up, 1)
                for x, name in enumerate("kv"):
                    for lh in range(2):
                        dve.tensor_scalar(wpos[:, x, lh, :], cc_("sub_rows"), sm("pos" + name)[:, lh:lh + 1], None, ALU.mult)
                    for g in range(2):
                        rows = slice(g * DH, g * DH + DH)
                        dve.tensor_copy(w1b[rows, x, rows], sm("w1" + name)[rows, :])
                        dve.tensor_copy(w2b[rows, x, rows], sm("w2" + name)[rows, :])
                for g in range(2):
                    rows, o = slice(g * DH, g * DH + DH), g * DH
                    dve.tensor_copy(w2b[rows, 2, o:o + 8], sm("w2k")[rows, 8:16])
                    dve.tensor_copy(w2b[rows, 2, o + 8:o + 16], sm("w2k")[rows, 0:8])
                for n in range(12):
                    s = 1.0 if n < 4 else DH ** -0.5
                    tile = rope_tile[n]
                    dve.wait_ge(swapped, n + 1)
                    dve.drain()
                    dve.scalar_tensor_tensor(out=t2[:, 0:TP], in0=ps[:, 6, :], scalar=s, in1=cc_("tok_sin")[:, 0:TP],
                                             op0=ALU.mult, op1=ALU.mult)
                    dve.scalar_tensor_tensor(out=t2[:, TP:NT], in0=ps[:, 7, 0:NS], scalar=s, in1=cc_("tok_sin")[:, TP:NT],
                                             op0=ALU.mult, op1=ALU.mult)
                    dve.scalar_tensor_tensor(out=tile, in0=tile, scalar=s, in1=cc_("tok_cos"), op0=ALU.mult, op1=ALU.mult)
                    dve.drain()
                    dve.tensor_tensor(tile, tile, t2, ALU.add).then_inc(roped, 1)
                dve.drain()
                dve.tensor_copy(knew, kk[:, :, TP:NT])
                for gp in range(2):
                    for g2 in range(2):
                        for r in range(R):
                            row = (2 * gp + g2) * 32 + r
                            rows = slice(g2 * DH, g2 * DH + DH)
                            dve.tensor_copy(qblk[rows, gp, :, row:row + 4 * TS - 3:4],
                                            qT[rows, gp * 4 + r, TP:NT].rearrange("p (b t) -> p b t", b=NB))
                dve.wait_ge(proj_evac, u0c + len(plan_c))
                dve.tensor_tensor(gates, gates, sm("b_gate").unsqueeze(1).to_broadcast([P, 5, 48]), ALU.add).then_inc(gate_sum, 1)

        def compress_dve_pool(dve, n):
            return dve.tensor_tensor(pooled[:, :, 0:n], lohi[:, :, 0, 0:n], lohi[:, :, 1, 1:n + 1], ALU.add)

        def compress_pe_hidden(pe, x, n, bank):
            return pe.matmul(ps[:, bank, 0:2 * n].rearrange("p (c n) -> p c n", c=2), w1b[:, x, :], pooled[:, 2 * x:2 * x + 2, 0:n],
                             start=True, stop=True)

        def compress_act_hidden(act, x, n, bank):
            return act.activation(hid[:, 2 * x:2 * x + 2, 0:n], ps[:, bank, 0:2 * n].rearrange("p (c n) -> p c n", c=2),
                                  ACT.Gelu_apprx_tanh, bias=sm("b1kv"[:2] + "kv"[x])[:, 0:1])

        def compress_pe_keys(pe, n, bank, bank2):
            pe.matmul(ps[:, bank, 0:2 * n].rearrange("p (c n) -> p c n", c=2), w2b[:, 0, :], hid[:, 0:2, 0:n], start=True, stop=True)
            return pe.matmul(ps[:, bank2, 0:2 * n].rearrange("p (c n) -> p c n", c=2), w2b[:, 2, :], hid[:, 0:2, 0:n],
                             start=True, stop=True)

        def compress_pe_values(pe, n, bank):
            for lo in range(0, n, P):
                m = min(P, n - lo)
                for half in range(2):
                    o = (lo // P) * KVW + half * P
                    last = pe.matmul(ps[0:m, bank, o:o + P], hid[:, 2 + half, lo:lo + m], w2b[:, 1, :], start=True, stop=True)
            return last

        def compress_dve_keys(dve, n, bank, bank2):
            cos = cd("cmp_cos")[:, 0:n].unsqueeze(1).to_broadcast([P, 2, n])
            sin = cd("cmp_sin")[:, 0:n].unsqueeze(1).to_broadcast([P, 2, n])
            a = ps[:, bank, 0:2 * n].rearrange("p (c n) -> p c n", c=2)
            b = ps[:, bank2, 0:2 * n].rearrange("p (c n) -> p c n", c=2)
            dve.tensor_tensor(kcT[:, :, 0:n], a, cos, ALU.mult)
            dve.tensor_tensor(ktmp[:, :, 0:n], b, sin, ALU.mult)
            dve.drain()
            return dve.tensor_tensor(kcT[:, :, 0:n], kcT[:, :, 0:n], ktmp[:, :, 0:n], ALU.add)

        pe_p, act_p, dve_p = sem("pe_pcmp"), sem("act_pcmp"), sem("dve_pcmp")
        PE2 = Order(["pool", "gates", "hidk", "hidv", "kc", "vc"])
        AC2 = Order(["hk", "hv", "vcs"])
        DV2 = Order(["lohi", "pooled", "kcT", "gates"])
        with nc.Block() as block:
            @block.tensor
            def _(pe):
                for c in range(4):
                    for t in range(4):
                        out = ps[:, 0, c * P:(c + 1) * P].rearrange("p (l n) -> p l n", l=2)[:, :, t * 8:t * 8 + 8]
                        last = pe.matmul(out, ccz[:, t, c * P:c * P + P], wpos[:, c // 2], start=True, stop=True)
                last.then_inc(pe_p, PE2.one("pool"))
                rt = cc_("row_token", NS).rearrange("p (b n) -> p b n", b=NB)
                for b in range(NB):
                    last = pe.matmul(ps[:, 2, b * 48:b * 48 + 48], rt[:, b, :], gates[0:NS, 4, :], start=True, stop=True)
                last.then_inc(pe_p, PE2.one("gates"))
                pe.wait_ge(dve_p, DV2["pooled"])
                compress_pe_hidden(pe, 0, NCMP_P, 1).then_inc(pe_p, PE2.one("hidk"))
                compress_pe_hidden(pe, 1, NCMP_P, 7).then_inc(pe_p, PE2.one("hidv"))
                pe.wait_ge(act_p, AC2["hv"])
                compress_pe_keys(pe, NCMP_P, 3, 4).then_inc(pe_p, PE2.one("kc"))
                compress_pe_values(pe, NCMP_P, 5).then_inc(pe_p, PE2.one("vc"))

            @block.scalar
            def _(act):
                act.wait_ge(pe_p, PE2["hidk"])
                compress_act_hidden(act, 0, NCMP_P, 1).then_inc(act_p, AC2.one("hk"))
                act.wait_ge(pe_p, PE2["hidv"])
                compress_act_hidden(act, 1, NCMP_P, 7).then_inc(act_p, AC2.one("hv"))
                act.wait_ge(pe_p, PE2["vc"])
                act.activation(vcs[0:NCMP_P, 0, :], ps[0:NCMP_P, 5, 0:KVW], ACT.Copy).then_inc(act_p, AC2.one("vcs"))

            @block.vector
            def _(dve):
                dve.wait_ge(pe_p, PE2["pool"])
                dve.tensor_copy(lohi[:, :, :, 0:32], ps[:, 0, :].rearrange("p (c l n) -> p c l n", c=4, l=2)[:, :, :, 0:32])\
                    .then_inc(dve_p, DV2.one("lohi"))
                dve.drain()
                compress_dve_pool(dve, NCMP_P).then_inc(dve_p, DV2.one("pooled"))
                dve.wait_ge(pe_p, PE2["kc"])
                compress_dve_keys(dve, NCMP_P, 3, 4).then_inc(dve_p, DV2.one("kcT"))
                dve.wait_ge(pe_p, PE2["gates"])
                dve.drain()
                g3_ = ktmp.rearrange("p c n -> p (c n)")[:, 0:NB * 48]
                g3 = g3_.rearrange("p (b c) -> p b c", b=NB)
                dve.tensor_tensor(g3, ps[:, 2, 0:NB * 48].rearrange("p (b c) -> p b c", b=NB),
                                  cc_("row_head").unsqueeze(1).to_broadcast([P, NB, 48]), ALU.mult)
                dve.drain()
                dve.tensor_reduce(grow, g3_.rearrange("p (b h c) -> p b c h", b=NB, c=3), AX.X, ALU.add)\
                    .then_inc(dve_p, DV2.one("gates"))

        ring_at = [0]

        def take_ring(cols):
            ring_at[0] += cols
            assert ring_at[0] <= RING * KT * CHUNK
            return wring_[:, ring_at[0] - cols:ring_at[0]]

        qs = take_ring(2 * TP).rearrange("p (c n) -> p c n", c=2)
        gs = take_ring(16 * 3).rearrange("p (t g c) -> p t g c", t=4, g=G)
        os_ = take_ring(16 * DH).rearrange("p (t g d) -> p t g d", t=4, g=G)
        pc = take_ring(16 * NCMP_P)
        pcs = take_ring(16)
        pcT = take_ring(4 * TP).rearrange("p (g n) -> p g n", g=G)
        Pb = take_ring(2 * TP).rearrange("p (s n) -> p s n", s=2)
        PTb = take_ring(2 * TP).rearrange("p (s n) -> p s n", s=2)
        nm = take_ring(4)
        sums = take_ring(4)
        rs = take_ring(4)
        units = [(g, t, br) for g in range(G) for t in range(4) for br in range(2)]
        U = len(units)
        pe_a, act_a, dve_a, tick = sem("pe_attn"), sem("act_attn"), sem("dve_attn"), sem("tick")
        names = ["cs"] + [("ct", g) for g in range(G)] + ["co0", "co1"]
        for i in range(U + 2):
            names += [("s", i)] * (i < U) + [("t", i - 1)] * (1 <= i <= U) + [("pv", i - 2)] * (i >= 2)
        PE3 = Order(names)
        names = ["cexp"] + [("ct", g) for g in range(G)] + ["co"]
        for i in range(U + 1):
            names += [("e", i)] * (i < U) + [("t", i - 1)] * (i >= 1)
        AC3 = Order(names)
        names = ["stage", "cmax", "cp"]
        for i in range(U + 3):
            names += [("m", i)] * (i < U) + [("o", i - 3)] * (i >= 3)
        DV3 = Order(names + ["end"])

        def at3(order, r, name, back=0):
            return (r + (1 - back)) * len(order) + order[name]

        def settle(eng):
            eng.sem_inc(tick, 1)

        with nc.Block() as block:
            @block.tensor
            def _(pe):
                pe.sem_inc(pe_a, len(PE3))
                with pe.Fori(0, R) as r:
                    pe.wait_ge(dve_a, at3(DV3, r, "stage"))
                    settle(pe)
                    pe.wait_ge(act_a, at3(AC3, r, ("t", U - 1), 1))
                    settle(pe)
                    for g in range(G):
                        rows, gp = slice((g % 2) * DH, (g % 2) * DH + DH), g // 2
                        for t in range(4):
                            o = (gp * 4 + t) * NCMP_P
                            last = pe.matmul(ps[:, 6 + g % 2, o:o + NCMP_P], qs[rows, gp, t * P:t * P + P], kcT[rows, gp, 0:NCMP_P],
                                             start=True, stop=True)
                    last.then_inc(pe_a, PE3.one("cs"))
                    pe.wait_ge(dve_a, at3(DV3, r, "cp"))
                    settle(pe)
                    for g in range(G):
                        for t in range(4):
                            o = (g * 4 + t) * NCMP_P
                            last = pe.transpose(ps[0:NCMP_P, g, t * P:t * P + P], pc[:, o:o + NCMP_P], ident)
                        last.then_inc(pe_a, PE3.one(("ct", g)))
                    for g2 in range(2):
                        pe.wait_ge(act_a, at3(AC3, r, ("ct", 2 * g2 + 1)))
                        settle(pe)
                        for g in (2 * g2, 2 * g2 + 1):
                            for t in range(4):
                                o = (g % 2) * 256 + t * DH
                                last = pe.matmul(ps[:, 4 + g2, o:o + DH], pcT[0:NCMP_P, g, t * P:t * P + P],
                                                 vcs[0:NCMP_P, 0, g * DH:g * DH + DH], start=True, stop=True)
                        last.then_inc(pe_a, PE3.one("co%d" % g2))
                    pe.wait_ge(act_a, at3(AC3, r, "co"))
                    settle(pe)
                    for i in range(U + 2):
                        if i < U:
                            g, t, br = units[i]
                            rows, gp = slice((g % 2) * DH, (g % 2) * DH + DH), g // 2
                            if i >= 3:
                                pe.wait_ge(act_a, at3(AC3, r, ("e", i - 3)))
                                settle(pe)
                            pe.matmul(ps[:, i % 3, 0:(t + 1) * P], qs[rows, gp, t * P:t * P + P],
                                      kk[rows, 2 * br + gp, 0:(t + 1) * P], start=True, stop=True).then_inc(pe_a, PE3.one(("s", i)))
                        if 1 <= i <= U:
                            g, t, br = units[i - 1]
                            pe.wait_ge(act_a, at3(AC3, r, ("e", i - 1)))
                            settle(pe)
                            for n in range(t + 1):
                                last = pe.transpose(ps[:, 3 + (i - 1) % 2, n * P:n * P + P], Pb[:, (i - 1) % 2, n * P:n * P + P], ident)
                            last.then_inc(pe_a, PE3.one(("t", i - 1)))
                        if i >= 2:
                            g, t, br = units[i - 2]
                            pe.wait_ge(act_a, at3(AC3, r, ("t", i - 2)))
                            settle(pe)
                            if i >= 4:
                                pe.wait_ge(dve_a, at3(DV3, r, ("o", i - 4)))
                                settle(pe)
                            for n in range(t + 1):
                                o = br * KVW + g * DH
                                last = pe.matmul(ps[:, 5 + i % 2, 0:DH], PTb[:, i % 2, n * P:n * P + P], vv[:, n, o:o + DH],
                                                 start=(n == 0), stop=(n == t))
                            last.then_inc(pe_a, PE3.one(("pv", i - 2)))

            @block.scalar
            def _(act):
                act.sem_inc(act_a, len(AC3))
                with act.Fori(0, R) as r:
                    act.wait_ge(dve_a, at3(DV3, r, "cmax"))
                    act.activation(pc, pc, ACT.Exp).then_inc(act_a, AC3.one("cexp"))
                    for g in range(G):
                        act.wait_ge(pe_a, at3(PE3, r, ("ct", g)))
                        act.activation(pcT[0:NCMP_P, g, :], ps[0:NCMP_P, g, :], ACT.Copy).then_inc(act_a, AC3.one(("ct", g)))
                    act.wait_ge(dve_a, at3(DV3, r, "end", 1))
                    settle(act)
                    for g2 in range(2):
                        act.wait_ge(pe_a, at3(PE3, r, "co%d" % g2))
                        last = act.activation(os_[:, :, 2 * g2:2 * g2 + 2, :].rearrange("p t g d -> p g t d"),
                                              ps[:, 4 + g2, :].rearrange("p (g t d) -> p g t d", g=2, t=4), ACT.Copy)
                    last.then_inc(act_a, AC3.one("co"))
                    for i in range(U + 1):
                        if i < U:
                            n = (units[i][1] + 1) * P
                            act.wait_ge(dve_a, at3(DV3, r, ("m", i)))
                            if i >= 2:
                                settle(act)
                                act.wait_ge(pe_a, at3(PE3, r, ("t", i - 2)))
                            act.activation(Pb[:, i % 2, 0:n], ps[:, i % 3, 0:n], ACT.Exp, bias=nm[:, i % 4:i % 4 + 1],
                                           accum_out=sums[:, i % 4:i % 4 + 1]).then_inc(act_a, AC3.one(("e", i)))
                        if i >= 1:
                            n = (units[i - 1][1] + 1) * P
                            act.wait_ge(pe_a, at3(PE3, r, ("t", i - 1)))
                            if i >= 3:
                                settle(act)
                                act.wait_ge(pe_a, at3(PE3, r, ("pv", i - 3)))
                            act.activation(PTb[:, (i - 1) % 2, 0:n], ps[:, 3 + (i - 1) % 2, 0:n], ACT.Copy)\
                                .then_inc(act_a, AC3.one(("t", i - 1)))

            @block.vector
            def _(dve):
                dve.sem_inc(dve_a, len(DV3))
                with dve.Fori(0, R) as r:
                    dve.wait_ge(pe_a, at3(PE3, r, ("s", U - 1), 1))
                    settle(dve)
                    for gp in range(2):
                        dve.tensor_scalar(qs[:, gp, :], qT[:, bass.ds(r + 4 * gp, 1), 0:TP].rearrange("p o n -> p (o n)"), 1.0, None, ALU.mult)
                    g5 = gates.rearrange("p t (g r c) -> p t g r c", g=G, r=R)
                    dve.tensor_scalar(gs, g5[:, 0:4, :, bass.ds(r, 1), :].rearrange("p t g r c -> p t g (r c)"), 1.0, None, ALU.mult)\
                        .then_inc(dve_a, DV3.one("stage"))
                    pc4 = pc.rearrange("p (g t n) -> p g t n", g=G, t=4)
                    pc3 = pc.rearrange("p (m n) -> p m n", n=NCMP_P)

                    def mask(name):
                        return cc_(name).unsqueeze(1).to_broadcast([P, G, 4 * NCMP_P])

                    pcg = pc.rearrange("p (g n) -> p g n", g=G)
                    dve.wait_ge(pe_a, at3(PE3, r, "cs"))
                    for g2 in range(2):
                        dve.tensor_tensor(pcg[:, g2::2], ps[:, 6 + g2, 0:8 * NCMP_P].rearrange("p (g n) -> p g n", g=2),
                                          mask("pcmp_add")[:, 0:2], ALU.add)
                    dve.drain()
                    dve.tensor_reduce(pcs, pc3, AX.X, ALU.max)
                    dve.drain()
                    dve.tensor_tensor(pc3, pc3, pcs.unsqueeze(2).to_broadcast([P, 16, NCMP_P]), ALU.subtract).then_inc(dve_a, DV3.one("cmax"))
                    dve.wait_ge(act_a, at3(AC3, r, "cexp"))
                    dve.tensor_tensor(pcg, pcg, mask("pcmp_keep"), ALU.mult)
                    dve.drain()
                    dve.tensor_reduce(pcs, pc3, AX.X, ALU.add)
                    dve.drain()
                    dve.tensor_scalar(pcs, pcs, 1e-30, None, ALU.max)
                    dve.drain()
                    dve.reciprocal(pcs, pcs)
                    dve.drain()
                    dve.tensor_tensor(pcs.rearrange("p (g t) -> p g t", g=G), pcs.rearrange("p (g t) -> p g t", g=G),
                                      gs[:, :, :, 0].rearrange("p t g -> p g t"), ALU.mult)
                    dve.drain()
                    dve.tensor_tensor(pc3, pc3, pcs.unsqueeze(2).to_broadcast([P, 16, NCMP_P]), ALU.mult).then_inc(dve_a, DV3.one("cp"))
                    for i in range(U + 3):
                        if i < U:
                            g, t, br = units[i]
                            dve.wait_ge(pe_a, at3(PE3, r, ("s", i)))
                            dve.tensor_tensor(ps[:, i % 3, t * P:t * P + P], ps[:, i % 3, t * P:t * P + P], cc_("causal_add"), ALU.add)
                            dve.drain()
                            dve.tensor_reduce(nm[:, i % 4:i % 4 + 1], ps[:, i % 3, 0:(t + 1) * P], AX.X, ALU.max, negate=True)\
                                .then_inc(dve_a, DV3.one(("m", i)))
                        if i >= 3:
                            j = i - 3
                            g, t, br = units[j]
                            c = j % 4
                            if j == 0:
                                dve.wait_ge(act_a, at3(AC3, r, "co"))
                                settle(dve)
                            dve.wait_ge(pe_a, at3(PE3, r, ("pv", j)))
                            settle(dve)
                            dve.wait_ge(act_a, at3(AC3, r, ("e", j)))
                            dve.reciprocal(rs[:, c:c + 1], sums[:, c:c + 1])
                            dve.drain()
                            dve.tensor_tensor(rs[:, c:c + 1], rs[:, c:c + 1], gs[:, t, g, 1 + br:2 + br], ALU.mult)
                            dve.drain()
                            dve.scalar_tensor_tensor(out=os_[:, t, g, :], in0=ps[:, 5 + j % 2, 0:DH], scalar=rs[:, c:c + 1],
                                                     in1=os_[:, t, g, :], op0=ALU.mult, op1=ALU.add).then_inc(dve_a, DV3.one(("o", j)))
                    dve.drain()
                    for t in range(4):
                        last = dve.tensor_scalar(oP[:, t, :, bass.ds(r, 1), :].rearrange("p g r d -> p g (r d)"), os_[:, t], 1.0, None, ALU.mult)
                    last.then_inc(dve_a, DV3.one("end"))
                    dve.drain()

        turned, gated = sem("turned"), sem("gated")
        with nc.Block() as block:
            @block.tensor
            def _(pe):
                for k in range(KT):
                    for t in range(4):
                        o_tile = oP[:, t, k // 2].rearrange("p r d -> p (r d)")[:, (k % 2) * P:(k % 2) * P + P]
                        last = pe.transpose(ps[:, k, t * P:t * P + P], o_tile, ident)
                    last.then_inc(turned, 1)

            @block.vector
            def _(dve):
                for k in range(KT):
                    dve.wait_ge(turned, k + 1)
                    dve.tensor_tensor(zT[:, k, 0:TP], ps[:, k, :], zT[:, k, 0:TP], ALU.mult).then_inc(gated, 1)

        GP = 4
        NG = PAGES // GP
        top[0] = mark_c
        cring = take(2 * GP * 512).rearrange("p (s q c) -> p s q c", s=2, q=GP)
        assert top[0] <= mark_c + 4 * D
        top[0] = mark_cmp
        SS = take(PAST + NS + TP + NS)
        SNEW, SWIN, SWNEW = PAST, PAST + NS, PAST + NS + TP
        PTr = take(3 * TP).rearrange("p (s n) -> p s n", s=3)
        oS = take(NB * P).rearrange("p (b d) -> p b d", b=NB)
        q_cmp = take(2 * P).rearrange("p (c n) -> p c n", c=2)
        q_sel = take(2 * P).rearrange("p (c n) -> p c n", c=2)
        Pc = take(2 * P)
        PcT = take(2 * P).rearrange("p (t n) -> p t n", t=2)
        imp0, score, score2 = take(NSEL), take(NSEL), take(NSEL)
        best, best2 = take(8), take(8)
        drop_next, drop = take(NSEL), take(NSEL)
        oc_next, oc = take(DH), take(DH)
        new_add, gw, o_row = take(NS), take(3), take(DH)
        mxs, negmax, sums11, rsum = take(11), take(2), take(11), take(2)
        cstat = take(2)
        KR, VR = 3, NG + 1
        kring = wring_[:, 0:KR * 1024].rearrange("p (s c) -> p s c", s=KR)
        vring = wring_[:, KR * 1024:(KR + VR) * 1024].rearrange("p (s n c) -> p s n c", s=VR, n=4)
        k_in = [sem(f"k_in{s}") for s in range(KR)]
        v_in = [sem(f"v_in{s}") for s in range(VR)]
        c_in = [sem(f"c_in{s}") for s in range(2)]
        win_out, win_stored = sem("win_out"), sem("win_stored")
        pe_s, act_s, dve_s = sem("pe_sel"), sem("act_sel"), sem("dve_sel")
        pe_c, act_c, dve_c = sem("pe_cmp"), sem("act_cmp"), sem("dve_cmp")
        tickp = sem("tickp")
        JS = list(range(NG)) + [NG + 1, NG]
        LAST = len(JS) - 1
        names = [("s", i) for i in range(NG + 2)]
        for n in range(len(JS) + 1):
            names += [("t", n)] * (n <= LAST) + [("pv", n - 1)] * (n >= 1)
        PS_ = Order(names)
        names = ["e0"]
        for n in range(len(JS)):
            names += ["e%d" % (n + 1)] * (n < LAST) + [("t", n)]
        AS_ = Order(names)
        DS_ = Order(["start"] + [("ev", i) for i in range(NG + 2)] + ["max", "out"])
        PC_ = Order([("pool", g) for g in range(NG)] + ["hidk", "hidv", "kc", "vc", "sc", "pt", "oc", "imp"])
        AC_ = Order(["hk", "hv", "vcs", "cexp", "pt"])
        DC_ = Order(["q"] + [("lohi", q) for q in range(NG // 2)] + ["pooled", "kc", "cmax", "cp", "imp0", "next"])

        def at4(order, n, name, back=0):
            return (n + (1 - back)) * len(order) + order[name]

        def k_value(n, i):
            per = [16 * (GP if j < NG else 1) for j in range(NG + 1)]
            return n * sum(per[i % KR::KR]) + sum(per[i % KR:i + 1:KR])

        def page_ids(eng, first):
            return nc.values_load_multi_w_load_instructions(pages[0:1, bass.ds(first, GP)], engines=[eng.engine],
                                                            min_val=0, max_val=v["selk_pages"].shape[0] - 1)[1]

        def load_keys(sp, n, i):
            if i == KR - 1:
                sp.wait_ge(win_stored, n + 1)
                settle_p(sp)
            sp.wait_ge(pe_s, at4(PS_, n, ("s", i - KR)) if i >= KR else at4(PS_, n, ("s", NG + 1 - KR + i), 1))
            settle_p(sp)
            if i == NG:
                sp.dma_start(kring[:, i % KR, :], v["win_k"][bass.ds(n, 1)].rearrange("o p c -> (o p) c")).then_inc(k_in[i % KR], 16)
                return
            for q, page in enumerate(page_ids(sp, n * PAGES + i * GP)):
                sp.dma_start(kring[:, i % KR, q * KVW:q * KVW + KVW],
                             v["selk_pages"][bass.ds(page, 1)].rearrange("o p c -> (o p) c")).then_inc(k_in[i % KR], 16)

        def load_cmp(sp, n, g):
            sp.wait_ge(pe_c, at4(PC_, n, ("pool", g - 2)) if g >= 2 else at4(PC_, n, ("pool", NG - 2 + g), 1))
            settle_p(sp)
            for q, page in enumerate(page_ids(sp, n * PAGES + g * GP)):
                sp.dma_start(cring[:, g % 2, q, :], v["cmp_pages"][bass.ds(page, 1)].rearrange("o p c -> (o p) c"))\
                    .then_inc(c_in[g % 2], 16)

        def settle_p(eng):
            eng.sem_inc(tick if eng is not nc.gpsimd else tickp, 1)

        def pe_pool(pe, n, g):
            pe.wait_ge(c_in[g % 2], n * (NG // 2 * 64) + 64 * (g // 2 + 1))
            settle(pe)
            if g % 2 == 0:
                pe.wait_ge(dve_c, at4(DC_, n, ("lohi", g // 2 - 1)) if g else at4(DC_, n, ("lohi", NG // 2 - 1), 1))
                settle(pe)
            for q in range(GP):
                for c in range(4):
                    out = ps[:, 0, c * P:(c + 1) * P].rearrange("p (l n) -> p l n", l=2)[:, :, (g % 2) * 32 + q * 8:(g % 2) * 32 + q * 8 + 8]
                    last = pe.matmul(out, cring[:, g % 2, q, c * P:c * P + P], wpos[:, c // 2], start=True, stop=True)
            last.then_inc(pe_c, PC_.one(("pool", g)))

        def pe_hidden(pe, n):
            pe.wait_ge(dve_c, at4(DC_, n, "pooled"))
            settle(pe)
            compress_pe_hidden(pe, 0, NCMP, 1).then_inc(pe_c, PC_.one("hidk"))
            compress_pe_hidden(pe, 1, NCMP, 7).then_inc(pe_c, PC_.one("hidv"))

        def pe_keys(pe, n):
            pe.wait_ge(act_c, at4(AC_, n, "hv"))
            settle(pe)
            compress_pe_keys(pe, NCMP, 1, 7).then_inc(pe_c, PC_.one("kc"))
            compress_pe_values(pe, NCMP, 0).then_inc(pe_c, PC_.one("vc"))

        def pe_scores_c(pe, n):
            pe.wait_ge(dve_c, at4(DC_, n, "kc"))
            settle(pe)
            for gp in range(2):
                rows = slice(gp * DH, gp * DH + DH)
                last = pe.matmul(ps[rows, 1, 0:NCMP], q_cmp[:, gp, rows], kcT[:, gp, 0:NCMP], start=True, stop=True)
            last.then_inc(pe_c, PC_.one("sc"))

        def pe_probs_c(pe, n):
            pe.wait_ge(dve_c, at4(DC_, n, "cp"))
            settle(pe)
            pe.transpose(ps[:, 7, 0:P], Pc[:, 0:P], ident)
            pe.transpose(ps[0:NCMP - P, 7, P:2 * P], Pc[:, P:NCMP], ident).then_inc(pe_c, PC_.one("pt"))

        def pe_out_c(pe, n):
            pe.wait_ge(act_c, at4(AC_, n, "pt"))
            settle(pe)
            for t, m in ((0, P), (1, NCMP - P)):
                for g in range(G):
                    pe.matmul(ps[32 * g:32 * g + 32, 1, 0:DH], PcT[0:m, t, 32 * g:32 * g + 32], vcs[0:m, t, g * DH:g * DH + DH],
                              start=(t == 0), stop=(t == 1))
            for t, m in ((0, P), (1, NCMP - P)):
                last = pe.matmul(ps[:, 7, 256:256 + NSEL], PcT[0:m, t, :], cd("overlap", m)[:, t * NSEL:(t + 1) * NSEL],
                                 start=(t == 0), stop=(t == 1))
            last.then_inc(pe_c, PC_.one("oc"))

        def pe_importance(pe, n):
            pe.wait_ge(dve_c, at4(DC_, n, "imp0"))
            settle(pe)
            pe.matmul(ps[:, 7, 384:384 + NSEL], cd("rep_sum"), imp0, start=True, stop=True).then_inc(pe_c, PC_.one("imp"))

        def pe_scores(pe, n, i):
            if i == 0:
                pe.wait_ge(dve_s, at4(DS_, n, "start"))
                settle(pe)
            if i <= NG:
                pe.wait_ge(k_in[i % KR], k_value(n, i))
                settle(pe)
            if i >= 2:
                pe.wait_ge(dve_s, at4(DS_, n, ("ev", i - 2)))
                settle(pe)
            bank = ps[:, 2 + i % 2, :]
            if i <= NG:
                for gp in range(2):
                    if i < NG:
                        keys = kring[:, i % KR, :].rearrange("p (q c n) -> p c q n", q=GP, c=2)[:, gp]
                        out = bank[gp * DH:gp * DH + DH].rearrange("p (q n) -> p q n", q=GP)
                    else:
                        keys, out = kring[:, i % KR, gp * TP:gp * TP + TP], bank[gp * DH:gp * DH + DH]
                    last = pe.matmul(out, q_sel[:, gp, gp * DH:gp * DH + DH], keys, start=True, stop=True)
            else:
                for x in range(2):
                    for gp in range(2):
                        last = pe.matmul(bank[gp * DH:gp * DH + DH, x * NS:x * NS + NS], q_sel[:, gp, gp * DH:gp * DH + DH],
                                         knew[:, 2 * x + gp, :], start=True, stop=True)
            last.then_inc(pe_s, PS_.one(("s", i)))

        def pe_turn(pe, n, at):
            j = JS[at]
            pe.wait_ge(act_s, at4(AS_, n, "e%d" % at))
            settle(pe)
            if at >= 2:
                pe.wait_ge(act_s, at4(AS_, n, ("t", at - 2)))
                settle(pe)
            bank = ps[:, 4 + at % 2, :]
            if j == NG + 1:
                pe.transpose(bank[0:NS, 0:P], SS[:, SNEW:SNEW + NS], ident)
                last = pe.transpose(bank[0:NS, P:2 * P], SS[:, SWNEW:SWNEW + NS], ident)
            else:
                o = j * TP if j < NG else SWIN
                for q in range(4):
                    last = pe.transpose(bank[:, q * P:q * P + P], SS[:, o + q * P:o + q * P + P], ident)
            last.then_inc(pe_s, PS_.one(("t", at)))

        def pe_values(pe, n, at):
            j = JS[at]
            pe.wait_ge(act_s, at4(AS_, n, ("t", at)))
            settle(pe)
            if j <= NG:
                pe.wait_ge(v_in[j], (n + 1) * (64 if j < NG else 16))
                settle(pe)
            if at == 0:
                pe.wait_ge(dve_s, at4(DS_, n, "out", 1))
                settle(pe)
            pt = PTr[:, at % 3, :]

            def add(x, m, at_row, values, start, stop):
                for g in range(G):
                    rows, o = slice(32 * g, 32 * g + 32), at_row + 32 * g
                    last = pe.matmul(ps[rows, 6, x * DH:x * DH + DH], pt[0:m, o:o + 32], values[:, g * DH:g * DH + DH],
                                     start=start, stop=stop)
                return last

            if j == NG + 1:
                add(0, NS, 0, vv[0:NS, 4, 0:KVW], False, True)
                last = add(1, NS, P, vv[0:NS, 4, KVW:2 * KVW], True, False)
            else:
                for q in range(4):
                    last = add(0 if j < NG else 1, P, q * P, vring[:, j, q, :], j == 0 and q == 0, j == NG and q == 3)
            last.then_inc(pe_s, PS_.one(("pv", at)))

        def act_hidden(act, n):
            act.wait_ge(pe_c, at4(PC_, n, "hidk"))
            settle(act)
            compress_act_hidden(act, 0, NCMP, 1).then_inc(act_c, AC_.one("hk"))
            act.wait_ge(pe_c, at4(PC_, n, "hidv"))
            settle(act)
            compress_act_hidden(act, 1, NCMP, 7).then_inc(act_c, AC_.one("hv"))

        def act_values_c(act, n):
            act.wait_ge(pe_c, at4(PC_, n, "vc"))
            settle(act)
            act.activation(vcs[:, 0, :], ps[:, 0, 0:KVW], ACT.Copy)
            act.activation(vcs[0:NCMP - P, 1, :], ps[0:NCMP - P, 0, KVW:2 * KVW], ACT.Copy).then_inc(act_c, AC_.one("vcs"))

        def act_exp_c(act, n):
            act.wait_ge(dve_c, at4(DC_, n, "cmax"))
            settle(act)
            act.activation(Pc[:, 0:NCMP], ps[:, 1, 0:NCMP], ACT.Exp, bias=cstat[:, 0:1], accum_out=cstat[:, 1:2])\
                .then_inc(act_c, AC_.one("cexp"))

        def act_probs_c(act, n):
            act.wait_ge(pe_c, at4(PC_, n, "pt"))
            settle(act)
            act.activation(PcT[:, 0, :], ps[:, 7, 0:P], ACT.Copy)
            act.activation(PcT[0:NCMP - P, 1, :], ps[0:NCMP - P, 7, P:2 * P], ACT.Copy).then_inc(act_c, AC_.one("pt"))

        def act_exp(act, n, at):
            j = JS[at]
            if at == 0:
                act.wait_ge(dve_s, at4(DS_, n, "max"))
                settle(act)
            if j == NG + 1:
                parts = [(SNEW, NS, 0, NG), (SWNEW, NS, 1, NG + 2)]
            else:
                parts = [(j * TP, TP, 0, j) if j < NG else (SWIN, TP, 1, NG + 1)]
            for o, w, which, c in parts:
                last = act.activation(SS[:, o:o + w], SS[:, o:o + w], ACT.Exp, bias=negmax[:, which:which + 1],
                                      accum_out=sums11[:, c:c + 1])
            last.then_inc(act_s, AS_.one("e%d" % at))

        def act_turned(act, n, at):
            act.wait_ge(pe_s, at4(PS_, n, ("t", at)))
            settle(act)
            if at >= 3:
                act.wait_ge(pe_s, at4(PS_, n, ("pv", at - 3)))
                settle(act)
            if JS[at] == NG + 1:
                last = act.activation(PTr[0:NS, at % 3, 0:2 * P], ps[0:NS, 4 + at % 2, 0:2 * P], ACT.Copy)
            else:
                last = act.activation(PTr[:, at % 3, :], ps[:, 4 + at % 2, :], ACT.Copy)
            last.then_inc(act_s, AS_.one(("t", at)))

        def dve_queries(dve, n):
            dve.drain()
            for gp in range(2):
                last = dve.tensor_scalar(q_cmp[:, gp, :], qblk[:, gp, bass.ds(n, 1), :].rearrange("p o c -> p (o c)"), 1.0, None, ALU.mult)
            last.then_inc(dve_c, DC_.one("q"))

        def dve_lohi(dve, n, q):
            dve.wait_ge(pe_c, at4(PC_, n, ("pool", 2 * q + 1)))
            settle(dve)
            dve.tensor_copy(lohi[:, :, :, q * 64:q * 64 + 64], ps[:, 0, :].rearrange("p (c l n) -> p c l n", c=4, l=2))\
                .then_inc(dve_c, DC_.one(("lohi", q)))
            if q == NG // 2 - 1:
                dve.drain()
                compress_dve_pool(dve, NCMP).then_inc(dve_c, DC_.one("pooled"))

        def dve_keys(dve, n):
            dve.wait_ge(pe_c, at4(PC_, n, "kc"))
            settle(dve)
            compress_dve_keys(dve, NCMP, 1, 7).then_inc(dve_c, DC_.one("kc"))

        def dve_max_c(dve, n):
            dve.wait_ge(pe_c, at4(PC_, n, "sc"))
            settle(dve)
            dve.tensor_reduce(cstat[:, 0:1], ps[:, 1, 0:NCMP], AX.X, ALU.max, negate=True).then_inc(dve_c, DC_.one("cmax"))

        def dve_probs_c(dve, n):
            dve.wait_ge(act_c, at4(AC_, n, "cexp"))
            settle(dve)
            dve.tensor_scalar(cstat[:, 1:2], cstat[:, 1:2], 1e-30, None, ALU.max)
            dve.drain()
            dve.reciprocal(cstat[:, 1:2], cstat[:, 1:2])
            dve.drain()
            dve.tensor_scalar(Pc[:, 0:NCMP], Pc[:, 0:NCMP], cstat[:, 1:2], None, ALU.mult)
            dve.drain()
            dve.scalar_tensor_tensor(out=Pc[:, 0:NCMP], in0=Pc[:, 0:NCMP], scalar=TINY, in1=Pc[:, 0:NCMP],
                                     op0=ALU.is_ge, op1=ALU.mult).then_inc(dve_c, DC_.one("cp"))

        def dve_out_c(dve, n):
            dve.wait_ge(pe_c, at4(PC_, n, "oc"))
            settle(dve)
            dve.tensor_copy(imp0, ps[:, 7, 256:256 + NSEL]).then_inc(dve_c, DC_.one("imp0"))
            dve.tensor_copy(oc_next, ps[:, 1, 0:DH])

        def dve_select(dve, n):
            dve.wait_ge(pe_c, at4(PC_, n, "imp"))
            settle(dve)
            dve.tensor_tensor(score, ps[:, 7, 384:384 + NSEL], cd("force"), ALU.add)
            dve.drain()
            dve.max(best, score)
            dve.drain()
            dve.match_replace(score2, best, score, -1.0)
            dve.drain()
            dve.max(best2, score2)
            dve.drain()
            dve.match_replace(score, best2, score2, -1.0)
            dve.drain()
            dve.tensor_scalar(drop_next, score, 0.0, NEG, ALU.is_ge, ALU.mult).then_inc(dve_c, DC_.one("next"))

        def dve_start(dve, n):
            dve.drain()
            dve.tensor_copy(q_sel, q_cmp)
            dve.tensor_copy(drop, drop_next)
            dve.tensor_copy(oc, oc_next)
            dve.tensor_scalar(gw, grow[:, bass.ds(n, 1), :].rearrange("p o c -> p (o c)"), 1.0, None, ALU.mult)
            new3 = cd("new_add").rearrange("p (b s) -> p b s", b=NB)
            dve.tensor_scalar(new_add, new3[:, bass.ds(n, 1), :].rearrange("p o c -> p (o c)"), 1.0, None, ALU.mult)\
                .then_inc(dve_s, DS_.one("start"))
            dve.drain()

        def dve_scores(dve, n, i):
            bank = ps[:, 2 + i % 2, :]
            dve.wait_ge(pe_s, at4(PS_, n, ("s", i)))
            settle(dve)
            if i < NG:
                keep = drop[:, 8 * i:8 * i + 8].unsqueeze(2).to_broadcast([P, 8, 64])
                dve.tensor_tensor(SS[:, i * TP:i * TP + TP].rearrange("p (k n) -> p k n", k=8),
                                  bank.rearrange("p (k n) -> p k n", k=8), keep, ALU.add).then_inc(dve_s, DS_.one(("ev", i)))
                dve.drain()
                dve.tensor_reduce(mxs[:, i:i + 1], SS[:, i * TP:i * TP + TP], AX.X, ALU.max)
            elif i == NG:
                dve.tensor_tensor(SS[:, SWIN:SWIN + TP], bank, cd("win_add"), ALU.add).then_inc(dve_s, DS_.one(("ev", i)))
                dve.drain()
                dve.tensor_reduce(mxs[:, NG + 1:NG + 2], SS[:, SWIN:SWIN + TP], AX.X, ALU.max)
            else:
                dve.scalar_tensor_tensor(out=SS[:, SNEW:SNEW + NS], in0=bank[:, 0:NS], scalar=drop[:, NSEL - 1:NSEL], in1=new_add,
                                         op0=ALU.add, op1=ALU.add)
                dve.tensor_tensor(SS[:, SWNEW:SWNEW + NS], bank[:, NS:2 * NS], new_add, ALU.add).then_inc(dve_s, DS_.one(("ev", i)))
                dve.drain()
                dve.tensor_reduce(mxs[:, NG:NG + 1], SS[:, SNEW:SNEW + NS], AX.X, ALU.max)
                dve.tensor_reduce(mxs[:, NG + 2:NG + 3], SS[:, SWNEW:SWNEW + NS], AX.X, ALU.max)
                dve.drain()
                dve.tensor_reduce(negmax[:, 0:1], mxs[:, 0:NG + 1], AX.X, ALU.max, negate=True)
                dve.tensor_reduce(negmax[:, 1:2], mxs[:, NG + 1:NG + 3], AX.X, ALU.max, negate=True).then_inc(dve_s, DS_.one("max"))

        def dve_combine(dve, n):
            dve.wait_ge(pe_s, at4(PS_, n, ("pv", LAST)))
            settle(dve)
            dve.tensor_reduce(rsum[:, 0:1], sums11[:, 0:NG + 1], AX.X, ALU.add)
            dve.tensor_reduce(rsum[:, 1:2], sums11[:, NG + 1:NG + 3], AX.X, ALU.add)
            dve.tensor_scalar(o_row, oc, gw[:, 0:1], None, ALU.mult)
            dve.drain()
            dve.tensor_scalar(rsum, rsum, 1e-30, None, ALU.max)
            dve.drain()
            dve.reciprocal(rsum, rsum)
            dve.drain()
            dve.tensor_tensor(rsum, rsum, gw[:, 1:3], ALU.mult)
            for x in range(2):
                dve.drain()
                dve.scalar_tensor_tensor(out=o_row, in0=ps[:, 6, x * DH:x * DH + DH], scalar=rsum[:, x:x + 1],
                                         in1=o_row, op0=ALU.mult, op1=ALU.add)
            dve.drain()
            for x in range(2):
                last = dve.tensor_scalar(oS[:, bass.ds(n, 1), x * DH:x * DH + DH].rearrange("p o d -> p (o d)"), o_row, 1.0, None, ALU.mult)
            last.then_inc(dve_s, DS_.one("out"))

        with nc.Block() as block:
            @block.sync
            def _(sp):
                for g in range(NG):
                    load_cmp(sp, 0, g)

                def keys_and_cmp(n, cmp):
                    for i in range(KR):
                        load_keys(sp, n, i)
                    for i in range(KR, NG + 1):
                        if cmp and i == KR:
                            load_cmp(sp, n + 1, 0)
                            load_cmp(sp, n + 1, 1)
                        load_keys(sp, n, i)
                        if cmp:
                            load_cmp(sp, n + 1, i - 1)

                with sp.Fori(0, NB - 1) as b:
                    keys_and_cmp(b, True)
                keys_and_cmp(NB - 1, False)

            @block.gpsimd
            def _(pool):
                pool.sem_inc(win_stored, 1)
                with pool.Fori(0, NB) as b:
                    for j in range(NG):
                        pool.wait_ge(pe_s, at4(PS_, b, ("pv", j), 1))
                        settle_p(pool)
                        for q, page in enumerate(page_ids(pool, b * PAGES + j * GP)):
                            pool.dma_start(vring[:, j, q, :], v["selv_pages"][bass.ds(page, 1)].rearrange("o p c -> (o p) c"))\
                                .then_inc(v_in[j], 16)
                    pool.wait_ge(pe_s, at4(PS_, b, ("pv", LAST), 1))
                    settle_p(pool)
                    pool.dma_start(vring[:, NG].rearrange("p n c -> p (n c)"), v["win_v"][bass.ds(b, 1)].rearrange("o p c -> (o p) c"))\
                        .then_inc(v_in[NG], 16)
                    pool.wait_ge(v_in[NG], b * 16 + 16)
                    settle_p(pool)
                    pool.dma_start(v["win_v_out"][bass.ds(b, 1)].rearrange("o p c -> (o p) c"), vring[:, NG].rearrange("p n c -> p (n c)"))\
                        .then_inc(win_out, 16)
                    pool.wait_ge(k_in[NG % KR], k_value(b, NG))
                    settle_p(pool)
                    pool.dma_start(v["win_k_out"][bass.ds(b, 1)].rearrange("o p c -> (o p) c"), kring[:, NG % KR, :]).then_inc(win_out, 16)
                    pool.wait_ge(win_out, b * 32 + 32)
                    pool.sem_inc(win_stored, 1)

            @block.tensor
            def _(pe):
                pe.sem_inc(pe_s, len(PS_))
                pe.sem_inc(pe_c, len(PC_))

                def tail(n):
                    return [lambda: pe_hidden(pe, n), lambda: pe_keys(pe, n), lambda: pe_scores_c(pe, n),
                            lambda: pe_probs_c(pe, n), lambda: pe_out_c(pe, n), lambda: pe_importance(pe, n)]

                def sample(n, cmp):
                    for i in range(NG + 2):
                        if cmp and i < NG:
                            pe_pool(pe, n + 1, i)
                        pe_scores(pe, n, i)
                    steps = tail(n + 1) if cmp else []
                    for at in range(len(JS) + 1):
                        if steps:
                            steps.pop(0)()
                        if at <= LAST:
                            pe_turn(pe, n, at)
                        if at >= 1:
                            pe_values(pe, n, at - 1)

                for g in range(NG):
                    pe_pool(pe, 0, g)
                for step in tail(0):
                    step()
                with pe.Fori(0, NB - 1) as b:
                    sample(b, True)
                sample(NB - 1, False)

            @block.scalar
            def _(act):
                act.sem_inc(act_s, len(AS_))
                act.sem_inc(act_c, len(AC_))

                def tail(n):
                    return [lambda: act_hidden(act, n), lambda: act_values_c(act, n), lambda: act_exp_c(act, n), lambda: act_probs_c(act, n)]

                def sample(n, cmp):
                    steps = tail(n + 1) if cmp else []
                    if steps:
                        steps.pop(0)()
                    act_exp(act, n, 0)
                    for at in range(len(JS)):
                        if at < LAST:
                            act_exp(act, n, at + 1)
                        act_turned(act, n, at)
                        if steps and at >= 0:
                            steps.pop(0)()

                for step in tail(0):
                    step()
                with act.Fori(0, NB - 1) as b:
                    sample(b, True)
                sample(NB - 1, False)

            @block.vector
            def _(dve):
                dve.sem_inc(dve_s, len(DS_))
                dve.sem_inc(dve_c, len(DC_))

                def tail(n):
                    for f in (dve_keys, dve_max_c, dve_probs_c, dve_out_c, dve_select):
                        f(dve, n)

                def sample(n, cmp):
                    dve_start(dve, n)
                    if cmp:
                        dve_queries(dve, n + 1)
                    for i in range(NG + 2):
                        dve_scores(dve, n, i)
                        if cmp and i % 2 == 1 and i < NG:
                            dve_lohi(dve, n + 1, i // 2)
                    if cmp:
                        tail(n + 1)
                    dve_combine(dve, n)
                    dve.drain()

                dve_queries(dve, 0)
                for q in range(NG // 2):
                    dve_lohi(dve, 0, q)
                tail(0)
                with dve.Fori(0, NB - 1) as b:
                    sample(b, True)
                sample(NB - 1, False)

        so_turned, so_gated = sem("so_turned"), sem("so_gated")
        with nc.Block() as block:
            @block.tensor
            def _(pe):
                for b in range(NB):
                    pe.transpose(ps[:, b, 0:P], oS[:, b, :], ident).then_inc(so_turned, 1)

            @block.vector
            def _(dve):
                for b in range(NB):
                    dve.wait_ge(so_turned, b + 1)
                    for rh in range(2):
                        for r2 in range(2):
                            rows = slice(r2 * DH, r2 * DH + DH)
                            got = ps[rows, b, 0:P].rearrange("p (g t r) -> p g t r", g=G, t=TS)
                            z = zT[rows, rh:KT:2, TP + b * TS:TP + b * TS + TS]
                            last = dve.tensor_tensor(z, got[:, :, :, 2 * rh + r2], z, ALU.mult)
                    last.then_inc(so_gated, 1)

        top[0] = mark_c
        sqf = take(KT * NT)
        stdF = take(NT)
        f_sq, f_sum, f_root, f_out = sem("f_squared"), sem("f_summed"), sem("f_rooted"), sem("f_out")
        with nc.Block() as block:
            @block.sync
            def _(sp):
                send_weights(sp, W_END)
                sp.wait_ge(f_out, 2)
                store(sp, v["y"].rearrange("p (k n) -> p k n", k=KT)[:, 0:4], sqf.rearrange("p (k n) -> p k n", k=KT)[:, 0:4])
                store(sp, v["y"].rearrange("p (k n) -> p k n", k=KT)[:, 4:8], sqf.rearrange("p (k n) -> p k n", k=KT)[:, 4:8])
                sp.wait_ge(outs, n_outs[0])

            @block.tensor
            def _(pe):
                project(pe, "co", plan_co, [zT[:, k, :] for k in range(KT)], None)
                pe.wait_ge(f_sq, KT)
                sq = sqf.rearrange("p (k n) -> p k n", k=KT)
                for k in range(KT):
                    pe.matmul(ps[:, 6, :], ones, sq[:, k, 0:TP], start=(k == 0), stop=(k == KT - 1))
                for k in range(KT):
                    last = pe.matmul(ps[:, 7, 0:NS], ones, sq[:, k, TP:NT], start=(k == 0), stop=(k == KT - 1))
                last.then_inc(f_sum, 1)

            @block.scalar
            def _(act):
                for k in range(KT):
                    act.wait_ge(proj_evac, first_unit["co"] + k + 1)
                    act.activation(sqf[:, k * NT:k * NT + NT], xT[:, k, :], ACT.Square).then_inc(f_sq, 1)
                act.wait_ge(f_sum, 1)
                act.activation(stdF[:, 0:TP], ps[:, 6, :], ACT.Sqrt, scale=1.0 / D, bias=eps[:, 0:1])
                act.activation(stdF[:, TP:NT], ps[:, 7, 0:NS], ACT.Sqrt, scale=1.0 / D, bias=eps[:, 0:1]).then_inc(f_root, 1)

            @block.vector
            def _(dve):
                residual(dve, "co", modC, 8)
                dve.drain()
                dve.wait_ge(f_root, 1)
                dve.reciprocal(stdF, stdF)
                dve.drain()
                sq = sqf.rearrange("p (k n) -> p k n", k=KT)
                for k in range(KT):
                    last = dve.scalar_tensor_tensor(out=sq[:, k], in0=xT[:, k], scalar=sm("final_norm")[:, k:k + 1], in1=stdF,
                                                    op0=ALU.mult, op1=ALU.mult)
                    if k % 4 == 3:
                        last.then_inc(f_out, 1)


def feature_pages(a):
    n, t = a.shape[:2]
    return a.reshape(n, t, 2, 2, DH).transpose(0, 3, 4, 2, 1).reshape(n, P, 2 * t)


def cmp_pages(v):
    return np.concatenate([v[f"cache_cmp_{x}"][0].reshape(-1, P, KVW) for x in "kv"], axis=2)


def kernel(**inputs):
    import concourse.bacc as bacc
    from concourse.bass_utils import run_bass_kernel_spmd

    v = {k: np.ascontiguousarray(np.asarray(a)) for k, a in inputs.items()}
    const = const_array()
    cut = CONST["tok_cos"][0]
    tokens = np.concatenate([v["x_prompt"][0], v["x_sample"].reshape(NS, D)], axis=0)
    arrays = {
        "small": small_array(v),
        "fixed": np.concatenate([np.eye(P), np.ones((P, P)), np.full((P, 1), EPS)], axis=1).astype(np.float32),
        "constA": const[:, :cut],
        "constC": const[:, cut:CONST["second part"]],
        "constD": const[:, CONST["second part"]:],
        "x": tokens.T.reshape(KT, P, NT).transpose(1, 0, 2).reshape(P, -1),
        "narrow": narrow_weights(v).reshape(P, -1),
        "pool_w": v["a_pool_w"][0].transpose(1, 0, 2).reshape(P, -1),
        "weights": weight_chunks(v),
        "page_table": v["page_table"].reshape(1, -1),
        "cmp_pages": cmp_pages(v),
        "selk_pages": feature_pages(v["cache_sel_k"][0]),
        "selv_pages": v["cache_sel_v"][0].reshape(-1, P, KVW),
        "win_k": feature_pages(v["cache_win_k"][0]),
        "win_v": v["cache_win_v"][0].reshape(NB, 4, P, KVW).transpose(0, 2, 1, 3).reshape(NB, P, 4 * KVW),
        "state_C": v["state_C"][0].transpose(2, 0, 1, 3).reshape(P, NB * H, HD),
    }
    outs = {"conv_out": (P, KT * 9 * 3), "pool_out": (P, 4 * 9 * 15), "C_s": (P, NB * H, HD), "C_p": (P, H, HD),
            "n_out": (P, 9 * H), "m_out": (H, 9),
            "cc_p": (P, 4, 512), "cc_s": (NS, 512), "vv_p": (P, 4, 512), "vv_s": (NS, 512), "kk": (P, 4, NT),
            "win_k_out": (NB, P, 2 * TP), "win_v_out": (NB, P, 4 * KVW), "y": (P, KT * NT)}
    nc = bacc.Bacc("TRN2", target_bir_lowering=False, num_devices=1)
    arrays = {n: np.ascontiguousarray(a) for n, a in arrays.items()}
    aps = {n: nc.dram_tensor("in_" + n, a.shape, mybir.dt.from_np(a.dtype), kind="ExternalInput").ap()
           for n, a in arrays.items()}
    aps.update({n: nc.dram_tensor("out_" + n, s, F32, kind="ExternalOutput").ap() for n, s in outs.items()})
    build(nc, aps)
    r = run_bass_kernel_spmd(nc, [{"in_" + n: a for n, a in arrays.items()}], core_ids=[0]).results[0]
    o = {n: r["out_" + n] for n in outs}

    def rows(a, n, j):
        a = a.reshape(P, n, 9, j).transpose(2, 3, 1, 0).reshape(9, j, n * P)
        return a[None, 0:1], a[None, 1:]

    y = o["y"].reshape(P, KT, NT).transpose(2, 1, 0).reshape(NT, D)
    pool_p, pool_s = rows(o["pool_out"], 4, 15)
    conv_p, conv_s = rows(o["conv_out"], KT, 3)
    n, m = o["n_out"], o["m_out"]
    res = [y[None, :TP], y[TP:].reshape(NB, TS, D), pool_p, pool_s, conv_p, conv_s,
           o["C_p"].transpose(1, 0, 2)[None, None], o["C_s"].reshape(P, NB, H, HD).transpose(1, 2, 0, 3)[None],
           n[:, :H].T[None, None], n[:, H:].reshape(P, NB, H).transpose(1, 2, 0)[None], m[:, 0][None, None], m[:, 1:].T[None]]

    def tokens_of(part, lo):
        p = o[part + "_p"][:, :, lo:lo + KVW].transpose(1, 0, 2).reshape(1, 1, TP, G, DH)
        return [p, o[part + "_s"][:, lo:lo + KVW].reshape(1, NB, TS, G, DH)]

    def keys(t):
        k = o["kk"][:, t:t + 2].reshape(2, DH, 2, NT).transpose(3, 2, 0, 1).reshape(NT, G, DH)
        return [k[None, None, :TP], k[TP:].reshape(1, NB, TS, G, DH)]

    res += tokens_of("cc", 0) + tokens_of("cc", KVW) + keys(0) + tokens_of("vv", 0)
    wk = o["win_k_out"].reshape(NB, 2, DH, 2, TP).transpose(0, 4, 3, 1, 2).reshape(1, NB, TP, G, DH)
    wv = o["win_v_out"].reshape(NB, P, 4, KVW).transpose(0, 2, 1, 3).reshape(1, NB, TP, G, DH)
    for new, old in ((keys(2), wk), (tokens_of("vv", KVW), wv)):
        res += [new[0], np.concatenate([old[:, :, TS:], new[1]], axis=2)]
    return tuple(np.ascontiguousarray(a) for a in res)
```
